# Optimizing a Trainium2 kernel written in Bass

```python
import math
import jax, jax.numpy as jnp
from jax import lax
import numpy as np

D_MODEL = 1024
BATCH = 1
SEQ = 1024
DEPTH = 2

HEAD_DIM = 64
A_HEADS = 4
A_WIDTH = A_HEADS * HEAD_DIM
A_PATTERNS = ((128, 1), (512, 4), (2048, 16))
B_HEADS = 6
B_KV_HEADS = 2
B_GROUP = B_HEADS // B_KV_HEADS
B_WIDTH = B_HEADS * HEAD_DIM
B_KV_WIDTH = B_KV_HEADS * HEAD_DIM
B_WINDOW = 128
B_BLOCK = 128
C_HEADS = 6
C_NOPE = 64
C_ROPE = 32
C_V = 64
C_WIDTH = C_HEADS * C_V
Q_LORA = 256
KV_LORA = 128
ROPE_THETA = 10000.0
C_QBLOCK = 128
D_MIX = A_WIDTH + B_WIDTH + C_WIDTH
IN_SPLITS = (A_WIDTH, A_WIDTH, A_WIDTH, A_WIDTH,
             B_WIDTH, B_KV_WIDTH, B_KV_WIDTH, B_WIDTH,
             Q_LORA, KV_LORA, C_ROPE, C_WIDTH)
D_IN = 4 * A_WIDTH + 2 * B_WIDTH + 2 * B_KV_WIDTH + Q_LORA + KV_LORA + C_ROPE + C_WIDTH
N_ALIBI = A_HEADS + B_HEADS
RMS_EPS = 1e-6
NEG_INF = -1e30

kernel_name = "hybrid_dilated_swa_mla_encoder"

def rmsnorm(x, g):
    xf = x.astype(jnp.float32)
    y = xf * lax.rsqrt(jnp.mean(xf * xf, axis=-1, keepdims=True) + RMS_EPS)
    return (y * g.astype(jnp.float32)).astype(x.dtype)

def split_cols(t, sizes):
    out, off = [], 0
    for s in sizes:
        out.append(t[..., off:off + s])
        off += s
    return out

def alibi_slopes():
    s = 2.0 ** (-8.0 * jnp.arange(1, N_ALIBI + 1, dtype=jnp.float32) / N_ALIBI)
    return s[B_HEADS:], s[:B_HEADS]

def rope(t, positions):
    half = C_ROPE // 2
    freq = ROPE_THETA ** (-2.0 * jnp.arange(half, dtype=jnp.float32) / C_ROPE)
    ang = positions.astype(jnp.float32)[..., None] * freq
    ang = ang.reshape(ang.shape[:2] + (1,) * (t.ndim - 3) + (half,))
    cos, sin = jnp.cos(ang), jnp.sin(ang)
    tf = t.astype(jnp.float32)
    t1, t2 = tf[..., :half], tf[..., half:]
    return jnp.concatenate([t1 * cos - t2 * sin, t1 * sin + t2 * cos], axis=-1).astype(t.dtype)

def _windows(t, blk, nb):
    return t

def banded_attention(q, k, v, half, blk, key_valid, dist_scale, slopes):
    *lead, hk, g, L, dh = q.shape
    nb = L // blk
    pad_kv = [(0, 0)] * (k.ndim - 2) + [(blk, blk), (0, 0)]
    kp = jnp.pad(k, pad_kv).reshape(k.shape[:-2] + (nb + 2, blk, dh))
    vp = jnp.pad(v, pad_kv).reshape(v.shape[:-2] + (nb + 2, blk, dh))
    kw = jnp.concatenate([kp[..., :-2, :, :], kp[..., 1:-1, :, :], kp[..., 2:, :, :]], axis=-2)
    vw = jnp.concatenate([vp[..., :-2, :, :], vp[..., 1:-1, :, :], vp[..., 2:, :, :]], axis=-2)
    valp = jnp.pad(key_valid, [(0, 0)] * (key_valid.ndim - 1) + [(blk, blk)], constant_values=False)
    valp = valp.reshape(key_valid.shape[:-1] + (nb + 2, blk))
    valw = jnp.concatenate([valp[..., :-2, :], valp[..., 1:-1, :], valp[..., 2:, :]], axis=-1)
    rel = jnp.arange(3 * blk)[None, :] - blk - jnp.arange(blk)[:, None]
    band = jnp.abs(rel) <= half
    bias = -slopes.astype(jnp.float32)[:, :, None, None, None] * (jnp.abs(rel) * dist_scale).astype(jnp.float32)
    qb = q.reshape(tuple(lead) + (hk, g, nb, blk, dh))
    s = jnp.einsum('...hgnqd,...hnkd->...hgnqk', qb, kw).astype(jnp.float32) * (dh ** -0.5) + bias
    mask = band & valw[..., None, None, :, None, :]
    s = jnp.where(mask, s, NEG_INF)
    m = jnp.max(s, axis=-1)
    p = jnp.exp(s - m[..., None])
    l = jnp.sum(p, axis=-1)
    acc = jnp.einsum('...hgnqk,...hnkd->...hgnqd', p, vw.astype(jnp.float32))
    shp = tuple(lead) + (hk, g, L)
    return m.reshape(shp), l.reshape(shp), acc.reshape(shp + (dh,))

def dilated_mixture(q, k, v, slopes_a):
    B, S, H, dh = q.shape
    ms, ls, accs = [], [], []
    for window, d in A_PATTERNS:
        half = window // (2 * d)
        blk = half
        chunk = d * blk
        Sp = ((S + chunk - 1) // chunk) * chunk
        L = Sp // d

        def to_res(t):
            t = jnp.pad(t, [(0, 0), (0, Sp - S), (0, 0), (0, 0)])
            return t.reshape(B, L, d, H, dh).transpose(0, 2, 3, 1, 4)

        qr, kr, vr = to_res(q)[:, :, :, None], to_res(k), to_res(v)
        valid = (jnp.arange(L)[None, :] * d + jnp.arange(d)[:, None]) < S
        m, l, acc = banded_attention(qr, kr, vr, half, blk, valid, d, slopes_a[:, None])
        ms.append(m[:, :, :, 0].transpose(0, 3, 1, 2).reshape(B, Sp, H)[:, :S])
        ls.append(l[:, :, :, 0].transpose(0, 3, 1, 2).reshape(B, Sp, H)[:, :S])
        accs.append(acc[:, :, :, 0].transpose(0, 3, 1, 2, 4).reshape(B, Sp, H, dh)[:, :S])
    M = jnp.maximum(jnp.maximum(ms[0], ms[1]), ms[2])
    es = [jnp.exp(m - M) for m in ms]
    num = es[0][..., None] * accs[0] + es[1][..., None] * accs[1] + es[2][..., None] * accs[2]
    den = es[0] * ls[0] + es[1] * ls[1] + es[2] * ls[2]
    out = num / den[..., None]
    return out.reshape(B, S, H * dh).astype(q.dtype)

def windowed_gqa_sink(q, k, v, sink, slopes_b):
    B, S, _, dh = q.shape
    qg = q.reshape(B, S, B_KV_HEADS, B_GROUP, dh).transpose(0, 2, 3, 1, 4)
    kg = k.transpose(0, 2, 1, 3)
    vg = v.transpose(0, 2, 1, 3)
    valid = jnp.ones((S,), dtype=bool)
    m, l, acc = banded_attention(qg, kg, vg, B_WINDOW, B_BLOCK, valid, 1,
                                 slopes_b.reshape(B_KV_HEADS, B_GROUP))
    sk = sink.astype(jnp.float32).reshape(B_KV_HEADS, B_GROUP)[:, :, None]
    M = jnp.maximum(m, sk)
    e = jnp.exp(m - M)
    den = l * e + jnp.exp(sk - M)
    out = acc * (e / den)[..., None]
    return out.transpose(0, 3, 1, 2, 4).reshape(B, S, B_WIDTH).astype(q.dtype)

def mla(cq, ckv, kr, positions, q_norm_g, kv_norm_g, w_uq, w_ukv):
    B, S, _ = cq.shape
    q = (rmsnorm(cq, q_norm_g) @ w_uq).reshape(B, S, C_HEADS, C_NOPE + C_ROPE)
    q_nope = q[..., :C_NOPE]
    q_rope = rope(q[..., C_NOPE:], positions)
    kv = (rmsnorm(ckv, kv_norm_g) @ w_ukv).reshape(B, S, C_HEADS, C_NOPE + C_V)
    k_nope = kv[..., :C_NOPE]
    v32 = kv[..., C_NOPE:].astype(jnp.float32)
    k_rope = rope(kr, positions)
    nq = S // C_QBLOCK
    qn = q_nope.reshape(B, nq, C_QBLOCK, C_HEADS, C_NOPE).swapaxes(0, 1)
    qr = q_rope.reshape(B, nq, C_QBLOCK, C_HEADS, C_ROPE).swapaxes(0, 1)
    scale = (C_NOPE + C_ROPE) ** -0.5

    def block(args):
        qn_b, qr_b = args
        s = (jnp.einsum('bqhd,bkhd->bhqk', qn_b, k_nope)
             + jnp.einsum('bqhd,bkd->bhqk', qr_b, k_rope)).astype(jnp.float32) * scale
        p = jax.nn.softmax(s, axis=-1)
        return jnp.einsum('bhqk,bkhd->bqhd', p, v32)

    o = lax.map(block, (qn, qr))
    return o.swapaxes(0, 1).reshape(B, S, C_WIDTH).astype(cq.dtype)

def setup_inputs(seed: int = 0) -> dict:
    key = jax.random.key(seed)
    ks = jax.random.split(key, 13)
    f32 = jnp.float32
    x = jax.random.normal(ks[0], (BATCH, SEQ, D_MODEL), f32)
    offset = jax.random.randint(ks[1], (BATCH, 1), 0, 1024, dtype=jnp.int32)
    positions = (offset + jnp.arange(SEQ, dtype=jnp.int32)[None, :]).astype(jnp.int32)
    pre_norm = 1.0 + 0.02 * jax.random.normal(ks[2], (DEPTH, D_MODEL), f32)
    w_in = jax.random.normal(ks[3], (DEPTH, D_MODEL, D_IN), f32) * D_MODEL ** -0.5
    q_a_norm = 1.0 + 0.02 * jax.random.normal(ks[4], (DEPTH, Q_LORA), f32)
    kv_a_norm = 1.0 + 0.02 * jax.random.normal(ks[5], (DEPTH, KV_LORA), f32)
    w_uq = jax.random.normal(ks[6], (DEPTH, Q_LORA, C_HEADS * (C_NOPE + C_ROPE)), f32) * Q_LORA ** -0.5
    w_ukv = jax.random.normal(ks[7], (DEPTH, KV_LORA, C_HEADS * (C_NOPE + C_V)), f32) * KV_LORA ** -0.5
    sink = 0.5 * jax.random.normal(ks[8], (DEPTH, B_HEADS), f32)
    w_o = jax.random.normal(ks[9], (DEPTH, D_MIX, D_MODEL), f32) * D_MIX ** -0.5
    post_norm = 1.0 + 0.02 * jax.random.normal(ks[10], (DEPTH, D_MODEL), f32)
    return {"x": x, "positions": positions, "pre_norm": pre_norm, "w_in": w_in,
            "q_a_norm": q_a_norm, "kv_a_norm": kv_a_norm, "w_uq": w_uq, "w_ukv": w_ukv,
            "sink": sink, "w_o": w_o, "post_norm": post_norm}

def reference(x, positions, pre_norm, w_in, q_a_norm, kv_a_norm, w_uq, w_ukv, sink, w_o, post_norm):
    B, S, _ = x.shape
    slopes_a, slopes_b = alibi_slopes()
    for i in range(DEPTH):
        h = rmsnorm(x, pre_norm[i])
        proj = h @ w_in[i]
        (qa, ka, va, ga, qb, kb, vb, gb, cq, ckv, kr, gc) = split_cols(proj, IN_SPLITS)
        ya = dilated_mixture(qa.reshape(B, S, A_HEADS, HEAD_DIM), ka.reshape(B, S, A_HEADS, HEAD_DIM),
                             va.reshape(B, S, A_HEADS, HEAD_DIM), slopes_a) * jax.nn.silu(ga)
        yb = windowed_gqa_sink(qb.reshape(B, S, B_HEADS, HEAD_DIM), kb.reshape(B, S, B_KV_HEADS, HEAD_DIM),
                               vb.reshape(B, S, B_KV_HEADS, HEAD_DIM), sink[i], slopes_b) * jax.nn.silu(gb)
        yc = mla(cq, ckv, kr, positions, q_a_norm[i], kv_a_norm[i], w_uq[i], w_ukv[i]) * jax.nn.silu(gc)
        y = jnp.concatenate([ya, yb, yc], axis=-1) @ w_o[i]
        x = x + rmsnorm(y, post_norm[i])
    return x


_drawn_inputs = setup_inputs


def setup_inputs(seed=0):
    import zlib

    import numpy as np

    out = dict(_drawn_inputs(seed))
    spreads = {}
    factors = {'q_a_norm': 8.0, 'kv_a_norm': 4.756, 'sink': 8.0}
    for name, (base, spread) in spreads.items():
        noise = np.random.default_rng([zlib.crc32(name.encode()), seed]).standard_normal(out[name].shape)
        drawn = base * np.exp(spread * noise) if base else spread * noise
        out[name] = __import__('jax').numpy.asarray(drawn.astype(out[name].dtype))
    for name, factor in factors.items():
        out[name] = (out[name] * factor).astype(out[name].dtype)
    return out
```

```python
import math
from contextlib import ExitStack

import concourse.bass as bass
import numpy as np
from concourse import mybir

ALU = mybir.AluOpType
ACT = mybir.ActivationFunctionType
AXES = mybir.AxisListType
F32 = mybir.dt.float32
F16 = mybir.dt.float16
I32 = mybir.dt.int32

P = 128
EPS = 1e-6
HEAD = 64
A_HEADS, B_HEADS, B_KV, C_HEADS = 4, 6, 2, 6
GROUP = 3
ROPE, HALF_ROPE = 32, 16
C_QK = HEAD + ROPE
Q_LORA, KV_LORA = 256, 128
PATTERNS = ((128, 1), (512, 4), (2048, 16))
B_WINDOW = 128
THETA = 10000.0
N_ALIBI = A_HEADS + B_HEADS
FAR = 1e30

W_SCALE = 32.0
UP_SCALE = 16.0


def alibi_slopes():
    s = 2.0 ** (-8.0 * np.arange(1, N_ALIBI + 1) / N_ALIBI)
    return s[B_HEADS:], s[:B_HEADS]


def penalty_tables(seq):
    slopes_a, slopes_b = alibi_slopes()
    rows = np.arange(P)[:, None]
    dist = np.abs(np.arange(2 * seq - P)[None, :] - (seq - P) - rows)
    times = sum(((dist % d == 0) & (dist <= w // 2)).astype(np.int64) for w, d in PATTERNS)
    log = np.log(np.maximum(times, 1))
    a = np.stack([np.where(times > 0, s * dist - log, FAR) for s in slopes_a], axis=1)
    near = np.abs(np.arange(3 * P)[None, :] - P - rows)
    b = np.stack([np.where(near <= B_WINDOW, s * near, FAR) for s in slopes_b], axis=1)
    return a.astype(np.float32), b.astype(np.float32)


def rope_frequencies():
    return (THETA ** (-2.0 * np.arange(HALF_ROPE) / ROPE)).astype(np.float32)


def encoder_kernel(nc, x, positions, pre_norm, w_in, q_a_norm, kv_a_norm, w_uq, w_ukv, sink, w_o, post_norm,
                   table_a, table_b, freq, eye, out):
    DEPTH, D, D_IN = w_in.shape
    SEQ = x.shape[1]
    TILES = SEQ // P
    KT = D // P
    SPAN = 2 * SEQ - P
    A_W, B_W, C_W = A_HEADS * HEAD, B_HEADS * HEAD, C_HEADS * HEAD
    assert SEQ == 1024 and D == 1024 and TILES == KT == 8

    CUTS = [0, 512, 1024, 1536, 2048, 2464, 2848]
    CHUNKS = 6
    assert CUTS[-1] == D_IN
    GATE = {1: (A_W, A_W, 0), 3: (2 * HEAD, B_W, A_W), 5: (0, C_W, A_W + B_W)}
    GROUPS = 8
    PROJ = CHUNKS * GROUPS

    PIECES = [("in", c, h) for c in range(CHUNKS) for h in range(2)] + [("up", 6, 0)]
    PIECES += [("out", c, h) for c in (7, 8) for h in range(2)]
    NP = len(PIECES)
    FIRST_PIECE = {c: min(i for i, p in enumerate(PIECES) if p[1] == c) for c in range(9)}
    UQ = C_HEADS * C_QK
    UKV = C_HEADS * 2 * HEAD
    UP_COLS = 2 * UQ + UKV

    UNITS = [("A", t, h) for t in range(TILES) for h in range(A_HEADS)]
    UNITS += [("B", t, h) for t in range(TILES) for h in range(B_HEADS)]
    UNITS += [("C", t, h) for t in range(TILES) for h in range(C_HEADS)]
    NU = len(UNITS)
    FROM = {"A": 0, "B": TILES * A_HEADS, "C": TILES * (A_HEADS + B_HEADS)}
    UPTO = {"A": FROM["B"], "B": FROM["C"], "C": NU}

    def key_tiles(u):
        branch, t, _ = UNITS[u]
        return range(max(t - 1, 0), min(t + 2, TILES)) if branch == "B" else range(TILES)

    HALVES = []
    HALF_FROM = []
    for u in range(NU):
        HALF_FROM.append(len(HALVES))
        tiles = list(key_tiles(u))
        HALVES += [(u, n, tiles[4 * n:4 * n + 4]) for n in range((len(tiles) + 3) // 4)]
    HALF_FROM.append(len(HALVES))
    NH = len(HALVES)

    def heads_of(u):
        return A_HEADS if UNITS[u][0] == "A" else GROUP

    OUT_GROUPS = []
    u = 0
    while u < NU:
        OUT_GROUPS.append((u, heads_of(u)))
        u += heads_of(u)
    NG = len(OUT_GROUPS)
    GROUP_OF = {u + i: g for g, (u, n) in enumerate(OUT_GROUPS) for i in range(n)}
    B_GROUPS = [g for g, (u, n) in enumerate(OUT_GROUPS) if UNITS[u][0] == "B"]
    SPLITS = [4, 12, 20, 28]
    KV_STEPS = 3 * 2 + TILES

    with ExitStack() as ctx:
        def sb(name, cols, dt=F32):
            return ctx.enter_context(nc.sbuf_tensor(name, [P, cols], dt))

        def sem(name):
            return ctx.enter_context(nc.semaphore(name))

        hT = sb("hT", 2 * KT * SEQ, F16)
        hT_hi = hT[:, 0:KT * SEQ].rearrange("p (k s) -> p k s", k=KT)
        hT_lo = hT[:, KT * SEQ:].rearrange("p (k s) -> p k s", k=KT)
        y_sb = sb("y", TILES * D)
        y = y_sb[:, :].rearrange("p (t d) -> p t d", t=TILES)
        stage_sb = sb("stage", 2 * 2048)
        stage = [stage_sb[:, 2048 * i:2048 * (i + 1)] for i in range(2)]
        wbuf = [sb(f"w{i}", 2 * KT * 512, F16) for i in range(2)]
        w_hi_of = [w[:, 0:KT * 512] for w in wbuf]
        w_lo_of = [w[:, KT * 512:] for w in wbuf]
        z = sb("z", 32 * 1024 // 4 + A_HEADS * SPAN)
        pp = sb("pp", 4096)
        scratch = sb("scratch", 2 * UQ)
        g_pre = sb("g_pre", D)
        g_post = sb("g_post", D)
        g_lat = sb("g_lat", Q_LORA + KV_LORA)
        cos = sb("cos", TILES * HALF_ROPE)
        sin = sb("sin", TILES * HALF_ROPE)
        ident = sb("ident", P)
        sinks = sb("sinks", DEPTH * B_HEADS)
        sink_now = sb("sink_now", B_HEADS)
        neg_sink = sb("neg_sink", B_HEADS)
        low = sb("low", NU)
        mass = sb("mass", NU)
        shift = sb("shift", GROUP * 2)
        sunk = sb("sunk", GROUP * 2)
        total = sb("total", 2 * 4)
        inverse = sb("inverse", 2 * 4)
        stat = sb("stat", 8 * TILES)
        lat_stat = sb("lat_stat", 6 * TILES)
        eps_col = sb("eps_col", 1)

        zh = z[:, :].bitcast(F16)

        def zpart(start_bytes, shape, rows=P):
            n = int(np.prod(shape))
            v = zh[0:rows, start_bytes // 2:start_bytes // 2 + n]
            names = "abcd"[:len(shape)]
            return v.rearrange(f"p ({' '.join(names)}) -> p {' '.join(names)}",
                               **{k: s for k, s in zip(names[:-1], shape[:-1])})

        K1 = 1024
        q_a = zpart(0, [A_HEADS, SEQ])
        k_a = [zpart(8 * K1, [A_HEADS, SEQ]), zpart(16 * K1, [A_HEADS, SEQ])]
        v_a = zpart(24 * K1, [TILES, A_HEADS, 2 * HEAD])
        tab_a = z[:, 8192:8192 + A_HEADS * SPAN].rearrange("p (h s) -> p h s", h=A_HEADS)
        q_b = zpart(0, [B_HEADS, SEQ])
        k_b = [zpart(12 * K1, [B_KV, SEQ]), zpart(16 * K1, [B_KV, SEQ])]
        v_b = zpart(20 * K1, [TILES, B_KV, 2 * HEAD])
        tab_b = z[:, 8192:8192 + B_HEADS * 3 * P].rearrange("p (h s) -> p h s", h=B_HEADS)
        q_c = [zpart(0, [C_HEADS, SEQ]), zpart(12 * K1, [C_HEADS, SEQ])]
        k_c = [zpart(24 * K1, [C_HEADS, SEQ]), zpart(36 * K1, [C_HEADS, SEQ])]
        v_c = zpart(48 * K1, [TILES, C_HEADS, 2 * HEAD])

        prob = [pp[:, 1024 * i:1024 * (i + 1)] for i in range(2)]
        turned_sb = [[pp[:, 2048 + 1024 * i + 512 * j:2048 + 1024 * i + 512 * (j + 1)].bitcast(F16)
                      .rearrange("p (b q) -> p b q", q=P) for j in range(2)] for i in range(2)]
        xb = prob
        xn = [pp[:, 2048 + 1024 * i:2048 + 1024 * (i + 1)] for i in range(2)]
        lat = [pp[:, 1536 * i:1536 * (i + 1)].bitcast(F16).rearrange("p (k s) -> p k s", k=3) for i in range(2)]
        LAT = Q_LORA + KV_LORA + ROPE
        lat_f = [pp[:, 3072 + LAT * i:3072 + LAT * (i + 1)] for i in range(2)]
        qf = [scratch[:, UQ * i:UQ * (i + 1)].rearrange("p (h d) -> p h d", h=C_HEADS) for i in range(2)]
        o_tmp = [scratch[:, 256 * i:256 * (i + 1)] for i in range(2)]
        o_sum = [scratch[:, 512 + 256 * i:512 + 256 * (i + 1)] for i in range(2)]
        junk = scratch[:, 0:D]
        cos_v = cos[:, :].rearrange("p (t f) -> p t f", t=TILES)
        sin_v = sin[:, :].rearrange("p (t f) -> p t f", t=TILES)
        stat_v = stat[:, :].rearrange("p (k t) -> p k t", t=TILES)
        lat_stat_v = lat_stat[:, :].rearrange("p (k t c) -> p k t c", k=3, t=TILES)

        ps = ctx.enter_context(nc.psum_tensor("ps", [P, 8, 512], F32))

        def pair(b):
            return ps[:, b:b + 2, :]

        const_loaded = sem("const_loaded")
        piece_loaded = [sem("piece_loaded_even"), sem("piece_loaded_odd")]
        piece_hi, piece_lo = sem("piece_hi"), sem("piece_lo")
        gains_loaded, next_gain_loaded = sem("gains_loaded"), sem("next_gain_loaded")
        table_a_loaded, table_b_loaded = sem("table_a_loaded"), sem("table_b_loaded")
        x_loaded = [sem("x_loaded_even"), sem("x_loaded_odd")]
        x_stored = [sem("x_stored_even"), sem("x_stored_odd")]
        rope_loaded = sem("rope_loaded")
        EACH = TILES // 2

        setup, carried = sem("setup"), sem("carried")
        angle, trig_step = sem("angle"), sem("trig_step")
        trig = sem("trig")
        pre_sq, pre_root, pre_inv = sem("pre_sq"), sem("pre_root"), sem("pre_inv")
        xn_done, x_turned, hT_hi_done, hT_done = sem("xn_done"), sem("x_turned"), sem("hT_hi_done"), sem("hT_done")
        proj_done, proj_act, proj_dve = sem("proj_done"), sem("proj_act"), sem("proj_dve")
        k_lo_done = sem("k_lo_done")
        gate_one, gate_inv = sem("gate_one"), sem("gate_inv")
        gains_scaled, sinks_negated = sem("gains_scaled"), sem("sinks_negated")
        lat_sq, lat_root, lat_inv = sem("lat_sq"), sem("lat_root"), sem("lat_inv")
        lat_prod, lat_done, lat_turned, lat_hi, lat_lo = (sem("lat_prod"), sem("lat_done"), sem("lat_turned"),
                                                         sem("lat_hi"), sem("lat_lo"))
        rope_spread = sem("rope_spread")
        kv_done, kv_hi, kv_lo = sem("kv_done"), sem("kv_hi"), sem("kv_lo")
        uq_done, uq_copied, uq_prod, uq_roped = sem("uq_done"), sem("uq_copied"), sem("uq_prod"), sem("uq_roped")
        uq_turned, uq_hi, uq_lo = sem("uq_turned"), sem("uq_hi"), sem("uq_lo")
        scores_done, low_done, exp_done = sem("scores_done"), sem("low_done"), sem("exp_done")
        prob_turned, prob_hi, prob_lo = sem("prob_turned"), sem("prob_hi"), sem("prob_lo")
        pv_done, o_copied, o_summed, y_gated, y_done = (sem("pv_done"), sem("o_copied"), sem("o_summed"),
                                                       sem("y_gated"), sem("y_done"))
        sink_shifted, sink_exp, sink_added, mass_inv = (sem("sink_shifted"), sem("sink_exp"), sem("sink_added"),
                                                       sem("mass_inv"))
        y_turned, yT_hi_done, yT_done = sem("y_turned"), sem("yT_hi_done"), sem("yT_done")
        out_done, post_sq, post_root, post_inv = sem("out_done"), sem("post_sq"), sem("post_root"), sem("post_inv")
        post_done, x_summed = sem("post_done"), sem("x_summed")

        block = ctx.enter_context(nc.Block())
        x_d = x.rearrange("b (t p) d -> (b t) p d", p=P)
        out_d = out.rearrange("b (t p) d -> (b t) p d", p=P)
        w_in_d = w_in.rearrange("l (k p) n -> l p k n", p=P)
        w_o_d = w_o.rearrange("l (k p) n -> l p k n", p=P)
        w_uq_d = w_uq.rearrange("l (k p) n -> l p k n", p=P)

        def one(t, L):
            return t[bass.ds(L, 1)]

        def piece_shape(i):
            kind, c, h = PIECES[i]
            cols = CUTS[c + 1] - CUTS[c] if kind == "in" else 512
            return kind, c, h, cols

        def staged(i):
            kind, c, h, cols = piece_shape(i)
            if kind == "up":
                return stage[i % 2][:, 0:UP_COLS]
            return stage[i % 2][:, 0:4 * cols].rearrange("p (k n) -> p k n", k=4)

        LOADS = [sum(3 if p[0] == "up" else 1 for p in PIECES[i::2]) for i in range(2)]

        def loads_upto(i):
            return sum(3 if p[0] == "up" else 1 for p in PIECES[i % 2:i + 1:2])

        def split_of(i, parts):
            kind, c, h, cols = piece_shape(i)
            if kind == "up":
                return parts[c % 2][:, 0:UP_COLS]
            return parts[c % 2].rearrange("p (k n) -> p k n", k=KT)[:, 4 * h:4 * h + 4, 0:cols]

        def weights(c):
            return [w[c % 2].rearrange("p (k n) -> p k n", k=KT) for w in (w_hi_of, w_lo_of)]

        def carry(eng):
            eng.sem_inc(carried, 1)

        @block.sync
        def _(sp):
            sp.dma_start(ident[:, :], eye).then_inc(const_loaded, 16)
            sp.dma_start(g_pre[:, :], pre_norm[0:1, :].broadcast_to([P, D])).then_inc(const_loaded, 16)
            for t in range(TILES):
                if t >= 2:
                    sp.wait_ge(x_stored[t % 2], 16 * (t // 2))
                    sp.wait_ge(xn_done, t - 1)
                sp.dma_start(xb[t % 2], x_d[t]).then_inc(x_loaded[t % 2], 16)
                sp.wait_ge(x_loaded[t % 2], 16 * (t // 2 + 1))
                sp.dma_start(out_d[t], xb[t % 2]).then_inc(x_stored[t % 2], 16)
                if t == 0:
                    sp.dma_start(cos[:, :].rearrange("p (t f) -> p t f", t=TILES)[:, 0, :],
                                 freq[0:1, :].broadcast_to([P, HALF_ROPE])).then_inc(rope_loaded, 16)
                    sp.dma_start(sinks[:, :], sink.rearrange("l h -> (l h)").unsqueeze(0)
                                 .broadcast_to([P, DEPTH * B_HEADS])).then_inc(rope_loaded, 16)
                    sp.dma_start(low[:, 0:TILES].bitcast(I32), positions).then_inc(rope_loaded, 16)
            with sp.Fori(0, DEPTH) as L:
                def load_piece(i):
                    kind, c, h, cols = piece_shape(i)
                    n = L * NP + max(i, 1)
                    sp.wait_ge(piece_hi, n)
                    carry(sp)
                    sp.wait_ge(piece_lo, n)
                    carry(sp)
                    loaded = piece_loaded[i % 2]
                    if kind == "in":
                        sp.dma_start(staged(i), one(w_in_d, L)[0][:, 4 * h:4 * h + 4, CUTS[c]:CUTS[c + 1]]
                                     ).then_inc(loaded, 16)
                    elif kind == "out":
                        sp.dma_start(staged(i), one(w_o_d, L)[0][:, 4 * h:4 * h + 4, 512 * (c - 7):512 * (c - 6)]
                                     ).then_inc(loaded, 16)
                    else:
                        sp.dma_start(stage[i % 2][:, 0:2 * UQ].rearrange("p (k n) -> p k n", k=2),
                                     one(w_uq_d, L)[0]).then_inc(loaded, 16)
                        for part in range(2):
                            sp.dma_start(stage[i % 2][:, 2 * UQ + C_W * part:2 * UQ + C_W * (part + 1)]
                                         .rearrange("p (h d) -> p h d", d=HEAD),
                                         one(w_ukv, L)[0].rearrange("p (h c d) -> p c h d", c=2, d=HEAD)[:, part]
                                         ).then_inc(loaded, 16)

                load_piece(0)
                load_piece(1)
                sp.dma_start(tab_a, table_a).then_inc(table_a_loaded, 16)
                sp.dma_start(g_lat[:, 0:Q_LORA], one(q_a_norm, L)[0].unsqueeze(0).broadcast_to([P, Q_LORA])
                             ).then_inc(gains_loaded, 16)
                sp.dma_start(g_lat[:, Q_LORA:], one(kv_a_norm, L)[0].unsqueeze(0).broadcast_to([P, KV_LORA])
                             ).then_inc(gains_loaded, 16)
                sp.dma_start(g_post[:, :], one(post_norm, L)[0].unsqueeze(0).broadcast_to([P, D])
                             ).then_inc(gains_loaded, 16)
                for i in range(2, 8):
                    load_piece(i)
                sp.wait_ge(xn_done, TILES * L + TILES)
                carry(sp)
                sp.dma_start(g_pre[:, :], one(pre_norm[1:DEPTH + 1, :], L)[0].unsqueeze(0).broadcast_to([P, D])
                             ).then_inc(next_gain_loaded, 16)
                sp.wait_ge(low_done, L * NU + UPTO["A"])
                carry(sp)
                sp.dma_start(tab_b, table_b).then_inc(table_b_loaded, 16)
                for i in range(8, NP):
                    load_piece(i)
                sp.wait_ge(prob_turned, L * NH + NH)
                carry(sp)
                sp.wait_ge(pv_done, L * NU + NU)
                carry(sp)
                for parity in range(2):
                    sp.wait_ge(x_stored[parity], 16 * EACH * (L + 1))
                    carry(sp)
                for t in range(TILES):
                    if t >= 2:
                        sp.wait_ge(x_stored[t % 2], 16 * (EACH * (L + 1) + t // 2))
                        carry(sp)
                        sp.wait_ge(xn_done, TILES * (L + 1) + t - 1)
                        carry(sp)
                    sp.dma_start(xb[t % 2], out_d[t]).then_inc(x_loaded[t % 2], 16)
                    if t >= 1:
                        sp.wait_ge(x_summed, TILES * L + t)
                        carry(sp)
                        sp.dma_start(out_d[t - 1], xb[(t - 1) % 2]).then_inc(x_stored[(t - 1) % 2], 16)
                sp.wait_ge(x_summed, TILES * L + TILES)
                carry(sp)
                sp.dma_start(out_d[TILES - 1], xb[(TILES - 1) % 2]).then_inc(x_stored[(TILES - 1) % 2], 16)
                for parity in range(2):
                    sp.wait_ge(x_stored[parity], 16 * EACH * (L + 2))
                    carry(sp)
                sp.wait_ge(xn_done, TILES * (L + 2))
                carry(sp)
            for parity in range(2):
                sp.wait_ge(x_stored[parity], 16 * EACH * (DEPTH + 1))

        @block.gpsimd
        def _(pool):
            with pool.Fori(0, DEPTH) as L:
                def gates(c):
                    frm, width, to = GATE[c]
                    for g in range(GROUPS):
                        pool.wait_ge(proj_act, L * PROJ + GROUPS * c + g + 1)
                        carry(pool)
                        nc.gpsimd.tensor_scalar(y[:, g, to:to + width], y[:, g, to:to + width], 1.0, None,
                                                ALU.add).then_inc(gate_one, 1)

                def branch(name, base):
                    for g, (u0, n) in enumerate(OUT_GROUPS):
                        if UNITS[u0][0] != name:
                            continue
                        _, t, h0 = UNITS[u0]
                        cols = y[:, t, base + HEAD * h0:base + HEAD * (h0 + n)]
                        yv = cols.rearrange("p (h d) -> p h d", h=n)
                        pool.wait_ge(o_summed, L * NG + g + 1)
                        nc.gpsimd.tensor_tensor(cols, o_sum[g % 2][:, 0:HEAD * n], cols, ALU.mult
                                                ).then_inc(y_gated, 1)
                        pool.wait_ge(y_gated, L * NG + g + 1)
                        pool.wait_ge(mass_inv, L * NG + g + 1)
                        nc.gpsimd.tensor_tensor(yv, yv, inverse[:, 4 * (g % 2):4 * (g % 2) + n].unsqueeze(2)
                                                .broadcast_to([P, n, HEAD]), ALU.mult).then_inc(y_done, 1)

                gates(1)
                branch("A", 0)
                gates(3)
                branch("B", A_W)
                gates(5)
                branch("C", A_W + B_W)

        @block.scalar
        def _(act):
            act.wait_ge(setup, 1)

            def square_norm(n, src, t):
                nc.scalar.activation(junk, src, ACT.Square, accum_out=stat_v[:, 0, t:t + 1]).then_inc(pre_sq, 1)
                act.wait_ge(pre_sq, n + 1)
                nc.scalar.activation(stat_v[:, 1, t:t + 1], stat_v[:, 0, t:t + 1], ACT.Sqrt, bias=eps_col[:, 0:1],
                                     scale=1.0 / D).then_inc(pre_root, 1)

            def high_of_h(n, t):
                act.wait_ge(x_turned, n + 1)
                nc.scalar.copy(hT_hi[:, :, P * t:P * (t + 1)], pair(4).rearrange("p b (k q) -> p (b k) q", q=P)
                               ).then_inc(hT_hi_done, 1)

            for t in range(TILES):
                act.wait_ge(x_loaded[t % 2], 16 * (t // 2 + 1))
                if t >= 1:
                    act.wait_ge(pre_sq, t)
                square_norm(t, xb[t % 2], t)
                if t >= 1:
                    high_of_h(t - 1, t - 1)
            high_of_h(TILES - 1, TILES - 1)
            act.wait_ge(angle, 1)
            nc.scalar.activation(sin[:, :], low[:, 0:TILES * HALF_ROPE], ACT.Sin).then_inc(trig, 1)
            nc.scalar.activation(cos[:, :], mass[:, 0:TILES * HALF_ROPE], ACT.Sin).then_inc(trig, 1)
            act.wait_ge(trig, 2)
            nc.scalar.copy(eps_col[:, 0:1], eps_col[:, 0:1]).then_inc(piece_hi, 1)

            with act.Fori(0, DEPTH) as L:
                def split(i):
                    kind = PIECES[i][0]
                    act.wait_ge(piece_loaded[i % 2], 16 * (L * LOADS[i % 2] + loads_upto(i)))
                    nc.scalar.activation(split_of(i, w_hi_of), staged(i), ACT.Copy,
                                         scale=UP_SCALE if kind == "up" else W_SCALE).then_inc(piece_hi, 1)

                def project(c):
                    for g in range(GROUPS):
                        G = GROUPS * c + g
                        src = ps[:, G % 4, :]
                        act.wait_ge(proj_done, L * PROJ + G + 1)
                        if c in (0, 2):
                            s, j = divmod(g, 4)
                            tok = slice(512 * s, 512 * s + 512)
                            queries = j < (2 if c == 0 else 3)
                            for e in range(2):
                                if queries:
                                    dst = (q_a if c == 0 else q_b)[0:HEAD, 2 * j + e, tok]
                                    scale = -(HEAD ** -0.5) / W_SCALE
                                else:
                                    dst = (k_a if c == 0 else k_b)[0][0:HEAD, 2 * (j % 2) * (c == 0) + e, tok]
                                    scale = 1.0 / W_SCALE
                                last = nc.scalar.activation(dst, src[HEAD * e:HEAD * (e + 1), :], ACT.Copy,
                                                            scale=scale)
                            last.then_inc(proj_act, 1)
                        elif c == 4:
                            for k, (a, b) in enumerate(((0, Q_LORA), (Q_LORA, Q_LORA + KV_LORA))):
                                if k == 1 or g >= 1:
                                    act.wait_ge(lat_sq, L * 2 * TILES + 2 * g + k)
                                last = nc.scalar.activation(junk[:, a:b], src[:, a:b], ACT.Square,
                                                            scale=1.0 / (W_SCALE * math.sqrt(b - a)),
                                                            accum_out=lat_stat_v[:, 0, g, k:k + 1])
                                last.then_inc(lat_sq, 1)
                            act.wait_ge(lat_sq, L * 2 * TILES + 2 * g + 2)
                            nc.scalar.activation(lat_stat_v[:, 1, g, :], lat_stat_v[:, 0, g, :], ACT.Sqrt,
                                                 bias=eps_col[:, 0:1]).then_inc(proj_act, 1)
                            if g >= 1:
                                latents_high(g - 1)
                        else:
                            frm, width, to = GATE[c]
                            if c != 5:
                                dst = (v_a if c == 1 else v_b)[:, g, :, 0:HEAD]
                                nc.scalar.activation(dst, src[:, 0:frm].rearrange("p (h d) -> p h d", d=HEAD),
                                                     ACT.Copy, scale=1.0 / W_SCALE)
                            nc.scalar.activation(y[:, g, to:to + width], src[:, frm:frm + width], ACT.Exp,
                                                 scale=-1.0 / W_SCALE).then_inc(proj_act, 1)
                            if c == 5 and g == 0:
                                latents_high(TILES - 1)
                        if c < 5 and g in (2, 5):
                            split(FIRST_PIECE[c + 1] + (g == 5))
                        if c == 5 and g == 2:
                            split(FIRST_PIECE[6])

                def latents_high(t):
                    act.wait_ge(lat_turned, L * TILES + t + 1)
                    tok = slice(P * t, P * (t + 1))
                    src = ps[:, 4 + t % 2, :].rearrange("p (k q) -> p k q", q=P)
                    nc.scalar.copy(lat[0][:, :, tok], src[:, 0:3, :])
                    nc.scalar.copy(k_c[0][HEAD:C_QK, 0, tok], src[0:ROPE, 3, :]).then_inc(lat_hi, 1)

                def up():
                    for m in range(KV_STEPS):
                        src = ps[:, 6 + m % 2, :]
                        act.wait_ge(kv_done, L * KV_STEPS + m + 1)
                        if m < 6:
                            for e in range(2):
                                last = nc.scalar.activation(
                                    k_c[0][0:HEAD, 2 * (m // 2) + e, 512 * (m % 2):512 * (m % 2 + 1)],
                                    src[HEAD * e:HEAD * (e + 1), :], ACT.Copy, scale=1.0 / UP_SCALE)
                        else:
                            last = nc.scalar.activation(v_c[:, m - 6, :, 0:HEAD],
                                                        src[:, 0:C_W].rearrange("p (h d) -> p h d", d=HEAD),
                                                        ACT.Copy, scale=1.0 / UP_SCALE)
                        last.then_inc(kv_hi, 1)

                    def high_of_q(t):
                        act.wait_ge(uq_turned, L * TILES + t + 1)
                        src = pair(4).rearrange("p b (k q) -> p (b k) q", q=P)
                        nc.scalar.copy(q_c[0][0:C_QK, :, P * t:P * (t + 1)], src[0:C_QK, 0:C_HEADS, :]
                                       ).then_inc(uq_hi, 1)

                    for t in range(TILES):
                        act.wait_ge(uq_done, L * TILES + t + 1)
                        if t >= 2:
                            act.wait_ge(uq_turned, L * TILES + t - 1)
                        nc.scalar.activation(qf[t % 2].rearrange("p (b h) d -> p b (h d)", b=2),
                                             pair(2 * (t % 2))[:, :, 0:UQ // 2], ACT.Copy,
                                             scale=-(C_QK ** -0.5) / UP_SCALE).then_inc(uq_copied, 1)
                        if t >= 1:
                            high_of_q(t - 1)
                    high_of_q(TILES - 1)

                def exponentials(u):
                    branch = UNITS[u][0]
                    w = P * len(key_tiles(u))
                    act.wait_ge(low_done, L * NU + u + 1)
                    if branch == "C":
                        act.wait_ge(prob_turned, L * NH + HALF_FROM[u - 1])
                        src = pair(2 * (u % 2)).rearrange("p b n -> p (b n)")
                    else:
                        src = prob[u % 2][:, 0:w]
                    nc.scalar.activation(prob[u % 2][:, 0:w], src, ACT.Exp, scale=-1.0, bias=low[:, u:u + 1],
                                         accum_out=mass[:, u:u + 1]).then_inc(exp_done, 1)

                def high_of_prob(u):
                    for k in range(HALF_FROM[u], HALF_FROM[u + 1]):
                        _, half, tiles = HALVES[k]
                        act.wait_ge(prob_turned, L * NH + k + 1)
                        if half == 0 and u - 2 >= FROM[UNITS[u][0]]:
                            act.wait_ge(pv_done, L * NU + u - 1)
                        n = len(tiles)
                        nc.scalar.copy(turned_sb[u % 2][0][:, 4 * half:4 * half + n, :],
                                       ps[:, 4 + k % 2, 0:P * n].rearrange("p (b q) -> p b q", q=P)
                                       ).then_inc(prob_hi, 1)

                def group_out(g):
                    u0, n = OUT_GROUPS[g]
                    if g in B_GROUPS:
                        i = B_GROUPS.index(g)
                        act.wait_ge(sink_shifted, L * len(B_GROUPS) + i + 1)
                        nc.scalar.activation(sunk[:, GROUP * (g % 2):GROUP * (g % 2 + 1)],
                                             shift[:, GROUP * (g % 2):GROUP * (g % 2 + 1)], ACT.Exp
                                             ).then_inc(sink_exp, 1)
                    act.wait_ge(pv_done, L * NU + u0 + n)
                    if g >= 2:
                        act.wait_ge(o_summed, L * NG + g - 1)
                    nc.scalar.copy(o_tmp[g % 2][:, 0:HEAD * n].rearrange("p (h d) -> p h d", h=n),
                                   ps[:, 6 + g % 2, 0:P * n].rearrange("p (h d) -> p h d", h=n)[:, :, HEAD:]
                                   ).then_inc(o_copied, 1)

                def attend(branch):
                    first, last = FROM[branch], UPTO[branch]
                    exponentials(first)
                    for i in range(first, last):
                        high_of_prob(i)
                        if i + 1 < last:
                            exponentials(i + 1)
                        if branch == "C" and i - first in SPLITS:
                            split(FIRST_PIECE[7] + SPLITS.index(i - first))
                        for g, (u0, n) in enumerate(OUT_GROUPS):
                            if u0 + n - 1 == i - 2 and i - 2 >= first:
                                group_out(g)
                    for g, (u0, n) in enumerate(OUT_GROUPS):
                        if last - 2 <= u0 + n - 1 < last:
                            group_out(g)

                def finish():
                    def high_of_y(t):
                        act.wait_ge(y_turned, L * TILES + t + 1)
                        nc.scalar.activation(hT_hi[:, :, P * t:P * (t + 1)],
                                             pair(6).rearrange("p b (k q) -> p (b k) q", q=P), ACT.Copy,
                                             scale=1.0 / W_SCALE).then_inc(yT_hi_done, 1)

                    high_of_y(0)
                    for t in range(TILES):
                        if t + 1 < TILES:
                            high_of_y(t + 1)
                        act.wait_ge(out_done, L * TILES + t + 1)
                        act.wait_ge(pre_sq, TILES * (L + 1) + t)
                        nc.scalar.activation(junk.rearrange("p (b n) -> p b n", b=2), pair(2 * (t % 2)), ACT.Square,
                                             scale=1.0 / W_SCALE, accum_out=stat_v[:, 3, t:t + 1]
                                             ).then_inc(post_sq, 1)
                        act.wait_ge(post_sq, L * TILES + t + 1)
                        nc.scalar.activation(stat_v[:, 4, t:t + 1], stat_v[:, 3, t:t + 1], ACT.Sqrt,
                                             bias=eps_col[:, 0:1], scale=1.0 / D).then_inc(post_root, 1)
                        if t >= 1:
                            high_of_h(TILES * (L + 1) + t - 1, t - 1)
                        act.wait_ge(x_summed, TILES * L + t + 1)
                        square_norm(TILES * (L + 1) + t, xb[t % 2], t)
                    high_of_h(TILES * (L + 1) + TILES - 1, TILES - 1)

                split(0)
                split(1)
                project(0)
                project(1)
                attend("A")
                project(2)
                project(3)
                attend("B")
                project(4)
                project(5)
                up()
                attend("C")
                finish()

        @block.vector
        def _(dve):
            nc.vector.memset(eps_col[:, :], EPS).then_inc(setup, 1)

            def normalise(n, src, t):
                dve.wait_ge(pre_root, n + 1)
                nc.vector.reciprocal(stat_v[:, 2, t:t + 1], stat_v[:, 1, t:t + 1]).then_inc(pre_inv, 1)
                dve.wait_ge(pre_inv, n + 1)
                if not isinstance(n, int) or n >= 2:
                    dve.wait_ge(x_turned, n - 1)
                nc.vector.scalar_tensor_tensor(out=xn[t % 2], in0=src, scalar=stat_v[:, 2, t:t + 1], in1=g_pre[:, :],
                                               op0=ALU.mult, op1=ALU.mult).then_inc(xn_done, 1)

            def low_of_h(n, t):
                dve.wait_ge(hT_hi_done, n + 1)
                nc.vector.tensor_tensor(hT_lo[:, :, P * t:P * (t + 1)],
                                        pair(4).rearrange("p b (k q) -> p (b k) q", q=P),
                                        hT_hi[:, :, P * t:P * (t + 1)], ALU.subtract).then_inc(hT_done, 1)

            dve.wait_ge(const_loaded, 32)
            for t in range(TILES):
                normalise(t, xb[t % 2], t)
                if t >= 1:
                    low_of_h(t - 1, t - 1)
            low_of_h(TILES - 1, TILES - 1)

            step = [0]

            def then(ins):
                step[0] += 1
                ins.then_inc(trig_step, 1)
                dve.wait_ge(trig_step, step[0])

            dve.wait_ge(rope_loaded, 16 * 3)
            R = TILES * HALF_ROPE
            posf = stat[:, 0:TILES]
            then(nc.vector.tensor_copy(posf, low[:, 0:TILES].bitcast(I32)))
            ang = y_sb[:, 0:R]
            turns, rest = y_sb[:, R:2 * R], y_sb[:, 2 * R:3 * R]
            then(nc.vector.tensor_tensor(ang.rearrange("p (t f) -> p t f", t=TILES),
                                         posf.unsqueeze(2).broadcast_to([P, TILES, HALF_ROPE]),
                                         cos_v[:, 0:1, :].broadcast_to([P, TILES, HALF_ROPE]), ALU.mult))
            ROUND = 1.5 * 2.0 ** 23
            PARTS = []
            left = 2.0 * math.pi
            for bits in (9, 12):
                e = 2.0 ** (bits - 1 - math.floor(math.log2(left)))
                PARTS.append(math.floor(left * e) / e)
                left -= PARTS[-1]
            PARTS.append(float(np.float32(left)))
            for target, quarter in ((low, 0.0), (mass, 0.25)):
                then(nc.vector.tensor_scalar(turns, ang, 1.0 / (2.0 * math.pi), quarter, ALU.mult, ALU.add))
                then(nc.vector.tensor_scalar(turns, turns, ROUND, None, ALU.add))
                then(nc.vector.tensor_scalar(turns, turns, ROUND, None, ALU.subtract))
                src = ang
                for part in PARTS:
                    then(nc.vector.scalar_tensor_tensor(out=rest, in0=turns, scalar=-part, in1=src,
                                                        op0=ALU.mult, op1=ALU.add))
                    src = rest
                if quarter:
                    then(nc.vector.tensor_scalar(rest, rest, math.pi / 2, None, ALU.add))
                then(nc.vector.tensor_scalar(target[:, 0:R], rest, 3.1415925, -3.1415925, ALU.min, ALU.max))
            nc.vector.memset(shift[:, :], 0.0).then_inc(angle, 1)
            nc.vector.memset(sunk[:, :], 0.0).then_inc(piece_lo, 1)

            with dve.Fori(0, DEPTH) as L:
                def split(i):
                    kind = PIECES[i][0]
                    dve.wait_ge(piece_hi, L * NP + i + 2)
                    nc.vector.scalar_tensor_tensor(out=split_of(i, w_lo_of), in0=staged(i),
                                                   scalar=UP_SCALE if kind == "up" else W_SCALE,
                                                   in1=split_of(i, w_hi_of), op0=ALU.mult, op1=ALU.subtract
                                                   ).then_inc(piece_lo, 1)

                def low_part(dst, src, scale, high):
                    return nc.vector.scalar_tensor_tensor(out=dst, in0=src, scalar=scale, in1=high, op0=ALU.mult,
                                                          op1=ALU.subtract)

                def project(c):
                    for g in range(GROUPS):
                        G = GROUPS * c + g
                        src = ps[:, G % 4, :]
                        dve.wait_ge(proj_act, L * PROJ + G + 1)
                        if c in (0, 2):
                            s, j = divmod(g, 4)
                            tok = slice(512 * s, 512 * s + 512)
                            if j < (2 if c == 0 else 3):
                                q = q_a if c == 0 else q_b
                                for e in range(2):
                                    last = low_part(q[HEAD:P, 2 * j + e, tok], src[HEAD * e:HEAD * (e + 1), :],
                                                    -(HEAD ** -0.5) / W_SCALE, q[0:HEAD, 2 * j + e, tok])
                                last.then_inc(proj_dve, 1)
                            else:
                                ks = k_a if c == 0 else k_b
                                h0 = 2 * (j % 2) * (c == 0)
                                for e in range(2):
                                    last = low_part(ks[1][0:HEAD, h0 + e, tok], src[HEAD * e:HEAD * (e + 1), :],
                                                    1.0 / W_SCALE, ks[0][0:HEAD, h0 + e, tok])
                                last.then_inc(k_lo_done, 1)
                                nc.vector.tensor_copy(ks[0][HEAD:P, h0:h0 + 2, tok], ks[0][0:HEAD, h0:h0 + 2, tok])
                                dve.wait_ge(k_lo_done, L * 6 + (2 * s + j - 1 if c == 0 else 5 + s))
                                nc.vector.tensor_copy(ks[1][HEAD:P, h0:h0 + 2, tok], ks[1][0:HEAD, h0:h0 + 2, tok]
                                                      ).then_inc(proj_dve, 1)
                        elif c == 4:
                            t = g
                            nc.vector.reciprocal(lat_stat_v[:, 2, t, :], lat_stat_v[:, 1, t, :]).then_inc(lat_inv, 1)
                            f = lat_f[t % 2]
                            tmp = scratch[:, D:D + 4 * HALF_ROPE].rearrange("p (k f) -> p k f", k=4)
                            if t >= 2:
                                dve.wait_ge(lat_turned, L * TILES + t - 1)
                            if t >= 1:
                                dve.wait_ge(lat_done, L * TILES + t)
                            a, b = Q_LORA + KV_LORA, Q_LORA + KV_LORA + HALF_ROPE
                            for k, (col, table) in enumerate(((a, cos_v), (b, sin_v), (a, sin_v), (b, cos_v))):
                                last = nc.vector.scalar_tensor_tensor(
                                    out=tmp[:, k, :], in0=src[:, col:col + HALF_ROPE], scalar=1.0 / W_SCALE,
                                    in1=table[:, t, :], op0=ALU.mult, op1=ALU.mult)
                            last.then_inc(lat_prod, 1)
                            dve.wait_ge(lat_inv, L * TILES + t + 1)
                            for k, (p, q) in enumerate(((0, Q_LORA), (Q_LORA, a))):
                                last = nc.vector.scalar_tensor_tensor(
                                    out=f[:, p:q], in0=src[:, p:q], scalar=lat_stat_v[:, 2, t, k:k + 1],
                                    in1=g_lat[:, p:q], op0=ALU.mult, op1=ALU.mult)
                            last.then_inc(proj_dve, 1)
                            dve.wait_ge(lat_prod, L * TILES + t + 1)
                            nc.vector.tensor_tensor(f[:, a:b], tmp[:, 0, :], tmp[:, 1, :], ALU.subtract)
                            nc.vector.tensor_tensor(f[:, b:b + HALF_ROPE], tmp[:, 2, :], tmp[:, 3, :], ALU.add
                                                    ).then_inc(lat_done, 1)
                            if t >= 1:
                                latents_low(t - 1)
                        else:
                            frm, width, to = GATE[c]
                            if c != 5:
                                v = v_a if c == 1 else v_b
                                low_part(v[:, g, :, HEAD:], src[:, 0:frm].rearrange("p (h d) -> p h d", d=HEAD),
                                         1.0 / W_SCALE, v[:, g, :, 0:HEAD])
                            n = GROUPS * (c // 2) + g + 1
                            gate = y[:, g, to:to + width]
                            dve.wait_ge(gate_one, L * 3 * GROUPS + n)
                            nc.vector.reciprocal(gate, gate).then_inc(gate_inv, 1)
                            dve.wait_ge(gate_inv, L * 3 * GROUPS + n)
                            nc.vector.tensor_tensor(gate, src[:, frm:frm + width], gate, ALU.mult
                                                    ).then_inc(proj_dve, 1)
                            if c == 5 and g == 0:
                                latents_low(TILES - 1)
                        if c < 5 and g in (2, 5):
                            split(FIRST_PIECE[c + 1] + (g == 5))
                        if c == 5 and g == 2:
                            split(FIRST_PIECE[6])

                def latents_low(t):
                    dve.wait_ge(lat_hi, L * TILES + t + 1)
                    tok = slice(P * t, P * (t + 1))
                    src = ps[:, 4 + t % 2, :].rearrange("p (k q) -> p k q", q=P)
                    nc.vector.tensor_tensor(lat[1][:, :, tok], src[:, 0:3, :], lat[0][:, :, tok], ALU.subtract)
                    nc.vector.tensor_tensor(k_c[1][HEAD:C_QK, 0, tok], src[0:ROPE, 3, :], k_c[0][HEAD:C_QK, 0, tok],
                                            ALU.subtract).then_inc(lat_lo, 1)

                def up():
                    dve.wait_ge(lat_lo, L * TILES + TILES)
                    for part in range(2):
                        last = nc.vector.tensor_copy(
                            k_c[part][HEAD:C_QK, 1:C_HEADS, :],
                            k_c[part][HEAD:C_QK, 0:1, :].broadcast_to([ROPE, C_HEADS - 1, SEQ]))
                    last.then_inc(rope_spread, 1)
                    for m in range(KV_STEPS):
                        src = ps[:, 6 + m % 2, :]
                        dve.wait_ge(kv_hi, L * KV_STEPS + m + 1)
                        if m < 6:
                            tok = slice(512 * (m % 2), 512 * (m % 2 + 1))
                            for e in range(2):
                                h = 2 * (m // 2) + e
                                last = low_part(k_c[1][0:HEAD, h, tok], src[HEAD * e:HEAD * (e + 1), :],
                                                1.0 / UP_SCALE, k_c[0][0:HEAD, h, tok])
                        else:
                            last = low_part(v_c[:, m - 6, :, HEAD:],
                                            src[:, 0:C_W].rearrange("p (h d) -> p h d", d=HEAD), 1.0 / UP_SCALE,
                                            v_c[:, m - 6, :, 0:HEAD])
                        last.then_inc(kv_lo, 1)

                    def low_of_q(t):
                        dve.wait_ge(uq_hi, L * TILES + t + 1)
                        src = pair(4).rearrange("p b (k q) -> p (b k) q", q=P)
                        tok = slice(P * t, P * (t + 1))
                        nc.vector.tensor_tensor(q_c[1][0:C_QK, :, tok], src[0:C_QK, 0:C_HEADS, :],
                                                q_c[0][0:C_QK, :, tok], ALU.subtract).then_inc(uq_lo, 1)

                    for t in range(TILES):
                        f = qf[t % 2]
                        t1, t2 = f[:, :, HEAD:HEAD + HALF_ROPE], f[:, :, HEAD + HALF_ROPE:C_QK]
                        tmp = pp[:, 3072:3072 + 4 * C_HEADS * HALF_ROPE].rearrange("p (k h f) -> p k h f", k=4,
                                                                                   f=HALF_ROPE)
                        c_t = cos_v[:, t:t + 1, :].broadcast_to([P, C_HEADS, HALF_ROPE])
                        s_t = sin_v[:, t:t + 1, :].broadcast_to([P, C_HEADS, HALF_ROPE])
                        dve.wait_ge(uq_copied, L * TILES + t + 1)
                        if t >= 1:
                            dve.wait_ge(uq_roped, L * TILES + t)
                        for k, (part, table) in enumerate(((t1, c_t), (t2, s_t), (t1, s_t), (t2, c_t))):
                            last = nc.vector.tensor_tensor(tmp[:, k, :, :], part, table, ALU.mult)
                        last.then_inc(uq_prod, 1)
                        dve.wait_ge(uq_prod, L * TILES + t + 1)
                        nc.vector.tensor_tensor(t1, tmp[:, 0, :, :], tmp[:, 1, :, :], ALU.subtract)
                        nc.vector.tensor_tensor(t2, tmp[:, 2, :, :], tmp[:, 3, :, :], ALU.add).then_inc(uq_roped, 1)
                        if t >= 1:
                            low_of_q(t - 1)
                    low_of_q(TILES - 1)

                def lowest(u):
                    branch, t, h = UNITS[u]
                    tiles = key_tiles(u)
                    w = P * len(tiles)
                    dve.wait_ge(scores_done, L * NU + u + 1)
                    src = pair(2 * (u % 2)).rearrange("p b n -> p (b n)")[:, 0:w]
                    if branch == "C":
                        nc.vector.tensor_reduce(low[:, u:u + 1], src, AXES.X, ALU.min).then_inc(low_done, 1)
                        return
                    if u - 2 >= FROM[branch]:
                        dve.wait_ge(prob_turned, L * NH + HALF_FROM[u - 1])
                    if branch == "A":
                        at = SEQ - P - P * t
                        table, first = tab_a[:, h, at:at + w], FAR
                    else:
                        at = P * (tiles[0] - t + 1)
                        table, first = tab_b[:, h, at:at + w], neg_sink[:, h:h + 1]
                    carry(dve)
                    nc.vector.tensor_tensor_reduce(out=prob[u % 2][:, 0:w], in0=src, in1=table, scale=1.0,
                                                   scalar=first, op0=ALU.add, op1=ALU.min,
                                                   accum_out=low[:, u:u + 1]).then_inc(low_done, 1)

                def low_of_prob(u):
                    for k in range(HALF_FROM[u], HALF_FROM[u + 1]):
                        _, half, tiles = HALVES[k]
                        n = len(tiles)
                        dve.wait_ge(prob_hi, L * NH + k + 1)
                        nc.vector.tensor_tensor(turned_sb[u % 2][1][:, 4 * half:4 * half + n, :],
                                                ps[:, 4 + k % 2, 0:P * n].rearrange("p (b q) -> p b q", q=P),
                                                turned_sb[u % 2][0][:, 4 * half:4 * half + n, :], ALU.subtract
                                                ).then_inc(prob_lo, 1)

                def group_mass(g):
                    u0, n = OUT_GROUPS[g]
                    dst = inverse[:, 4 * (g % 2):4 * (g % 2) + n]
                    dve.wait_ge(exp_done, L * NU + u0 + n)
                    if g >= 2:
                        dve.wait_ge(y_done, L * NG + g - 1)
                    if g in B_GROUPS:
                        i = B_GROUPS.index(g)
                        h0 = UNITS[u0][2]
                        at = slice(GROUP * (g % 2), GROUP * (g % 2 + 1))
                        nc.vector.tensor_tensor(shift[:, at], low[:, u0:u0 + n], sink_now[:, h0:h0 + n], ALU.add
                                                ).then_inc(sink_shifted, 1)
                        dve.wait_ge(sink_exp, L * len(B_GROUPS) + i + 1)
                        nc.vector.tensor_tensor(total[:, 4 * (g % 2):4 * (g % 2) + n], mass[:, u0:u0 + n],
                                                sunk[:, at], ALU.add).then_inc(sink_added, 1)
                        dve.wait_ge(sink_added, L * len(B_GROUPS) + i + 1)
                        nc.vector.reciprocal(dst, total[:, 4 * (g % 2):4 * (g % 2) + n]).then_inc(mass_inv, 1)
                    else:
                        nc.vector.reciprocal(dst, mass[:, u0:u0 + n]).then_inc(mass_inv, 1)

                def group_out(g):
                    u0, n = OUT_GROUPS[g]
                    group_mass(g)
                    dve.wait_ge(o_copied, L * NG + g + 1)
                    nc.vector.tensor_tensor(o_sum[g % 2][:, 0:HEAD * n].rearrange("p (h d) -> p h d", h=n),
                                            ps[:, 6 + g % 2, 0:P * n].rearrange("p (h d) -> p h d", h=n)[:, :, 0:HEAD],
                                            o_tmp[g % 2][:, 0:HEAD * n].rearrange("p (h d) -> p h d", h=n), ALU.add
                                            ).then_inc(o_summed, 1)

                def attend(branch):
                    first, last = FROM[branch], UPTO[branch]
                    lowest(first)
                    lowest(first + 1)
                    for i in range(first, last):
                        low_of_prob(i)
                        if i + 2 < last:
                            lowest(i + 2)
                        if branch == "C" and i - first in SPLITS:
                            split(FIRST_PIECE[7] + SPLITS.index(i - first))
                        for g, (u0, n) in enumerate(OUT_GROUPS):
                            if u0 + n - 1 == i - 2 and i - 2 >= first:
                                group_out(g)
                    for g, (u0, n) in enumerate(OUT_GROUPS):
                        if last - 2 <= u0 + n - 1 < last:
                            group_out(g)

                def finish():
                    def low_of_y(t):
                        dve.wait_ge(yT_hi_done, L * TILES + t + 1)
                        low_part(hT_lo[:, :, P * t:P * (t + 1)], pair(6).rearrange("p b (k q) -> p (b k) q", q=P),
                                 1.0 / W_SCALE, hT_hi[:, :, P * t:P * (t + 1)]).then_inc(yT_done, 1)

                    dve.wait_ge(next_gain_loaded, 16 * (L + 1))
                    low_of_y(0)
                    for t in range(TILES):
                        if t + 1 < TILES:
                            low_of_y(t + 1)
                        dve.wait_ge(post_root, L * TILES + t + 1)
                        nc.vector.reciprocal(stat_v[:, 5, t:t + 1], stat_v[:, 4, t:t + 1]).then_inc(post_inv, 1)
                        dve.wait_ge(post_inv, L * TILES + t + 1)
                        if t == 0:
                            dve.wait_ge(pv_done, L * NU + NU)
                        else:
                            dve.wait_ge(x_turned, TILES * (L + 1) + t - 1)
                        nc.vector.scalar_tensor_tensor(out=xn[t % 2].rearrange("p (b n) -> p b n", b=2),
                                                       in0=pair(2 * (t % 2)), scalar=stat_v[:, 5, t:t + 1],
                                                       in1=g_post[:, :].rearrange("p (b n) -> p b n", b=2),
                                                       op0=ALU.mult, op1=ALU.mult).then_inc(post_done, 1)
                        dve.wait_ge(post_done, L * TILES + t + 1)
                        dve.wait_ge(x_loaded[t % 2], 16 * (EACH * (L + 1) + t // 2 + 1))
                        nc.vector.tensor_tensor(xb[t % 2], xb[t % 2], xn[t % 2], ALU.add).then_inc(x_summed, 1)
                        if t >= 1:
                            low_of_h(TILES * (L + 1) + t - 1, t - 1)
                        dve.wait_ge(x_summed, TILES * L + t + 1)
                        normalise(TILES * (L + 1) + t, xb[t % 2], t)
                    low_of_h(TILES * (L + 1) + TILES - 1, TILES - 1)

                split(0)
                split(1)
                dve.wait_ge(gains_loaded, 48 * (L + 1))
                nc.vector.tensor_scalar(g_lat[:, :], g_lat[:, :], 1.0 / W_SCALE, None, ALU.mult
                                        ).then_inc(gains_scaled, 1)
                nc.vector.tensor_scalar(g_post[:, :], g_post[:, :], 1.0 / W_SCALE, None, ALU.mult
                                        ).then_inc(gains_scaled, 1)
                now = sinks[:, :].rearrange("p (l h) -> p l h", h=B_HEADS)[:, bass.ds(L, 1), :]
                nc.vector.tensor_scalar(sink_now[:, :].unsqueeze(1), now, 1.0, None, ALU.mult).then_inc(sinks_negated, 1)
                nc.vector.tensor_scalar(neg_sink[:, :].unsqueeze(1), now, -1.0, None, ALU.mult
                                        ).then_inc(sinks_negated, 1)
                dve.wait_ge(gains_scaled, 2 * (L + 1))
                dve.wait_ge(sinks_negated, 2 * (L + 1))
                project(0)
                project(1)
                dve.wait_ge(table_a_loaded, 16 * (L + 1))
                attend("A")
                project(2)
                project(3)
                dve.wait_ge(table_b_loaded, 16 * (L + 1))
                attend("B")
                project(4)
                project(5)
                up()
                attend("C")
                finish()

        @block.tensor
        def _(pe):
            def turn_x(n, t):
                pe.wait_ge(xn_done, n + 1)
                if not isinstance(n, int) or n >= 1:
                    pe.wait_ge(hT_done, n)
                for k in range(KT):
                    last = nc.tensor.transpose(ps[:, 4 + k // 4, P * (k % 4):P * (k % 4 + 1)],
                                               xn[t % 2][:, P * k:P * (k + 1)], ident[:, :])
                last.then_inc(x_turned, 1)

            pe.wait_ge(const_loaded, 32)
            for t in range(TILES):
                turn_x(t, t)

            with pe.Fori(0, DEPTH) as L:
                def project(c):
                    n = CUTS[c + 1] - CUTS[c]
                    hi, lo = weights(c)
                    for g in range(GROUPS):
                        G = GROUPS * c + g
                        if c == 0:
                            pe.wait_ge(hT_done, TILES * L + 4 * (g // 4) + 4)
                        if G >= 4:
                            pe.wait_ge(proj_act, L * PROJ + G - 3)
                            pe.wait_ge(proj_dve, L * PROJ + G - 3)
                        dst = ps[:, G % 4, 0:n]
                        for k in range(KT):
                            if g == 0 and k % 4 == 0:
                                pe.wait_ge(piece_lo, L * NP + FIRST_PIECE[c] + k // 4 + 2)
                            if c in (0, 2):
                                s, j = divmod(g, 4)
                                tok, cols = slice(512 * s, 512 * s + 512), slice(P * j, P * (j + 1))
                                terms = ((hi[:, k, cols], hT_hi[:, k, tok]), (hi[:, k, cols], hT_lo[:, k, tok]),
                                         (lo[:, k, cols], hT_hi[:, k, tok]))
                            else:
                                tok = slice(P * g, P * (g + 1))
                                terms = ((hT_hi[:, k, tok], hi[:, k, 0:n]), (hT_hi[:, k, tok], lo[:, k, 0:n]),
                                         (hT_lo[:, k, tok], hi[:, k, 0:n]))
                            for m, (a, b) in enumerate(terms):
                                last = nc.tensor.matmul(dst, a, b, start=(k == 0 and m == 0),
                                                        stop=(k == KT - 1 and m == 2))
                        last.then_inc(proj_done, 1)
                        if c == 4 and g >= 1:
                            turn_latents(g - 1)
                        if c == 5 and g == 0:
                            turn_latents(TILES - 1)

                def turn_latents(t):
                    pe.wait_ge(lat_done, L * TILES + t + 1)
                    pe.wait_ge(proj_dve, L * PROJ + GROUPS * 4 + t + 1)
                    if t >= 2:
                        pe.wait_ge(lat_lo, L * TILES + t - 1)
                    for k in range(4):
                        w = ROPE if k == 3 else P
                        last = nc.tensor.transpose(ps[0:w, 4 + t % 2, P * k:P * (k + 1)],
                                                   lat_f[t % 2][:, P * k:P * k + w], ident[:, :])
                    last.then_inc(lat_turned, 1)

                def three(dst, a, b, first, last):
                    for m, (p, q) in enumerate(((a[0], b[0]), (a[0], b[1]), (a[1], b[0]))):
                        ins = nc.tensor.matmul(dst, p, q, start=(first and m == 0), stop=(last and m == 2))
                    return ins

                def up():
                    wq = [w[0][:, 0:2 * UQ].rearrange("p (k n) -> p k n", k=2) for w in (w_hi_of, w_lo_of)]
                    wkv = [w[0][:, 2 * UQ:UP_COLS].rearrange("p (c n) -> p c n", c=2)
                           for w in (w_hi_of, w_lo_of)]
                    pe.wait_ge(piece_lo, L * NP + FIRST_PIECE[6] + 2)
                    pe.wait_ge(lat_lo, L * TILES + TILES)
                    pe.wait_ge(proj_act, L * PROJ + PROJ)
                    pe.wait_ge(proj_dve, L * PROJ + PROJ)
                    for m in range(KV_STEPS):
                        if m >= 2:
                            pe.wait_ge(kv_hi, L * KV_STEPS + m - 1)
                            pe.wait_ge(kv_lo, L * KV_STEPS + m - 1)
                        dst = ps[:, 6 + m % 2, :]
                        if m < 6:
                            h, s = m // 2, m % 2
                            ins = three(dst, [w[:, 0, P * h:P * (h + 1)] for w in wkv],
                                        [v[:, 2, 512 * s:512 * (s + 1)] for v in lat], True, True)
                        else:
                            t = m - 6
                            ins = three(dst[:, 0:C_W],
                                        [v[:, 2, P * t:P * (t + 1)] for v in lat],
                                        [w[:, 1, :] for w in wkv], True, True)
                        ins.then_inc(kv_done, 1)

                    def turn_q(t):
                        pe.wait_ge(uq_roped, L * TILES + t + 1)
                        if t >= 1:
                            pe.wait_ge(uq_lo, L * TILES + t)
                        for h in range(C_HEADS):
                            last = nc.tensor.transpose(ps[0:C_QK, 4 + h // 4, P * (h % 4):P * (h % 4 + 1)],
                                                       qf[t % 2][:, h, :], ident[:, :])
                        last.then_inc(uq_turned, 1)

                    for t in range(TILES):
                        if t >= 2:
                            pe.wait_ge(uq_copied, L * TILES + t - 1)
                        for b in range(2):
                            for k in range(2):
                                ins = three(ps[:, 2 * (t % 2) + b, 0:UQ // 2],
                                            [v[:, k, P * t:P * (t + 1)] for v in lat],
                                            [w[:, k, UQ // 2 * b:UQ // 2 * (b + 1)] for w in wq], k == 0, k == 1)
                        ins.then_inc(uq_done, 1)
                        if t >= 1:
                            turn_q(t - 1)
                    turn_q(TILES - 1)

                def scores(u):
                    branch, t, h = UNITS[u]
                    tiles = key_tiles(u)
                    w = P * len(tiles)
                    if u - 2 >= FROM[branch]:
                        pe.wait_ge(exp_done if branch == "C" else low_done, L * NU + u - 1)
                    tok = slice(P * t, P * (t + 1))
                    for b in range((w + 511) // 512):
                        n = min(512, w - 512 * b)
                        keys = slice(P * tiles[0] + 512 * b, P * tiles[0] + 512 * b + n)
                        dst = ps[:, 2 * (u % 2) + b, 0:n]
                        if branch == "C":
                            last = three(dst, [q[0:C_QK, h, tok] for q in q_c], [k[0:C_QK, h, keys] for k in k_c],
                                         True, True)
                        else:
                            q, ks, kh = (q_a, k_a, h) if branch == "A" else (q_b, k_b, h // GROUP)
                            for m in range(2):
                                last = nc.tensor.matmul(dst, q[:, h, tok], ks[m][:, kh, keys], start=(m == 0),
                                                        stop=(m == 1))
                    last.then_inc(scores_done, 1)

                def turn(u):
                    pe.wait_ge(exp_done, L * NU + u + 1)
                    for k in range(HALF_FROM[u], HALF_FROM[u + 1]):
                        _, half, tiles = HALVES[k]
                        if k - 2 >= HALF_FROM[FROM[UNITS[u][0]]]:
                            pe.wait_ge(prob_lo, L * NH + k - 1)
                        for b in range(len(tiles)):
                            last = nc.tensor.transpose(ps[:, 4 + k % 2, P * b:P * (b + 1)],
                                                       prob[u % 2][:, 512 * half + P * b:512 * half + P * (b + 1)],
                                                       ident[:, :])
                        last.then_inc(prob_turned, 1)

                def values(u):
                    branch, t, h = UNITS[u]
                    g = GROUP_OF[u]
                    u0 = OUT_GROUPS[g][0]
                    v, vh = {"A": (v_a, h), "B": (v_b, h // GROUP), "C": (v_c, h)}[branch]
                    pe.wait_ge(prob_lo, L * NH + HALF_FROM[u + 1])
                    if u == u0 and g >= 2:
                        pe.wait_ge(o_summed, L * NG + g - 1)
                    hi, lo = turned_sb[u % 2]
                    dst = ps[:, 6 + g % 2, P * (u - u0):P * (u - u0 + 1)]
                    tiles = key_tiles(u)
                    for b, kt in enumerate(tiles):
                        def high_terms():
                            return nc.tensor.matmul(dst, hi[:, b, :], v[:, kt, vh, :], start=(b == 0),
                                                    stop=(b == len(tiles) - 1), skip_group_check=True)

                        def low_term():
                            nc.tensor.matmul(dst[:, 0:HEAD], lo[:, b, :], v[:, kt, vh, 0:HEAD], start=False,
                                             stop=False, skip_group_check=True)

                        if b < len(tiles) - 1:
                            high_terms()
                            low_term()
                        else:
                            low_term()
                            last = high_terms()
                    last.then_inc(pv_done, 1)

                def attend(branch):
                    first, last = FROM[branch], UPTO[branch]
                    scores(first)
                    scores(first + 1)
                    for i in range(first, last):
                        turn(i)
                        if i + 2 < last:
                            scores(i + 2)
                        if i - 1 >= first:
                            values(i - 1)
                    values(last - 1)
                    pe.wait_ge(o_summed, L * NG + GROUP_OF[last - 1] + 1)

                def finish():
                    whi, wlo = zip(weights(7), weights(8))

                    def turn_y(t):
                        if t == 0:
                            pe.wait_ge(y_done, L * NG + NG)
                        else:
                            pe.wait_ge(yT_done, L * TILES + t)
                        for k in range(KT):
                            last = nc.tensor.transpose(ps[:, 6 + k // 4, P * (k % 4):P * (k % 4 + 1)],
                                                       y[:, t, P * k:P * (k + 1)], ident[:, :])
                        last.then_inc(y_turned, 1)

                    turn_y(0)
                    pe.wait_ge(piece_lo, L * NP + NP + 1)
                    for t in range(TILES):
                        if t + 1 < TILES:
                            turn_y(t + 1)
                        pe.wait_ge(yT_done, L * TILES + t + 1)
                        if t >= 2:
                            pe.wait_ge(post_done, L * TILES + t - 1)
                        tok = slice(P * t, P * (t + 1))
                        for k in range(KT):
                            for m, (a, w) in enumerate(((hT_hi, whi), (hT_hi, wlo), (hT_lo, whi))):
                                for b in range(2):
                                    last = nc.tensor.matmul(ps[:, 2 * (t % 2) + b, :], a[:, k, tok], w[b][:, k, :],
                                                            start=(k == 0 and m == 0), stop=(k == KT - 1 and m == 2))
                        last.then_inc(out_done, 1)
                        if t >= 1:
                            turn_x(TILES * (L + 1) + t - 1, t - 1)
                    turn_x(TILES * (L + 1) + TILES - 1, TILES - 1)

                project(0)
                project(1)
                pe.wait_ge(proj_dve, L * PROJ + 2 * GROUPS)
                attend("A")
                project(2)
                project(3)
                pe.wait_ge(proj_dve, L * PROJ + 4 * GROUPS)
                attend("B")
                project(4)
                project(5)
                up()
                pe.wait_ge(rope_spread, L + 1)
                pe.wait_ge(kv_lo, L * KV_STEPS + KV_STEPS)
                pe.wait_ge(uq_lo, L * TILES + TILES)
                attend("C")
                finish()


_INS = ["x", "positions", "pre_norm", "w_in", "q_a_norm", "kv_a_norm", "w_uq", "w_ukv", "sink", "w_o", "post_norm"]


def kernel(**inputs):
    import concourse.bacc as _bacc
    from concourse.bass_utils import run_bass_kernel_spmd as _run

    nc = _bacc.Bacc("TRN2", target_bir_lowering=False, num_devices=1)
    data = {name: np.ascontiguousarray(inputs[name]) for name in _INS}
    data["pre_norm"] = np.concatenate([data["pre_norm"], data["pre_norm"][:1]])
    seq = data["x"].shape[1]
    data["positions"] = np.ascontiguousarray(data["positions"].reshape(seq // P, P).T)
    data["table_a"], data["table_b"] = penalty_tables(seq)
    data["freq"] = rope_frequencies()[None, :]
    data["eye"] = np.eye(P, dtype=np.float32)
    arrays, args = {}, []
    for name, a in data.items():
        arrays[f"in_{name}_dram"] = a
        args.append(nc.dram_tensor(f"in_{name}_dram", a.shape, mybir.dt.from_np(a.dtype), kind="ExternalInput").ap())
    args.append(nc.dram_tensor("out_0_dram", data["x"].shape, F32, kind="ExternalOutput").ap())
    encoder_kernel(nc, *args)
    r = _run(nc, [arrays], core_ids=[0])
    return r.results[0]["out_0_dram"]
```

```python
import math
from contextlib import ExitStack

import concourse.bass as bass
import numpy as np
from concourse import mybir

ALU = mybir.AluOpType
ACT = mybir.ActivationFunctionType
AXES = mybir.AxisListType
F32 = mybir.dt.float32
F16 = mybir.dt.float16
I32 = mybir.dt.int32

P = 128
EPS = 1e-6
HEAD = 64
A_HEADS, B_HEADS, B_KV, C_HEADS = 4, 6, 2, 6
GROUP = 3
ROPE, HALF_ROPE = 32, 16
C_QK = HEAD + ROPE
Q_LORA, KV_LORA = 256, 128
PATTERNS = ((128, 1), (512, 4), (2048, 16))
B_WINDOW = 128
THETA = 10000.0
N_ALIBI = A_HEADS + B_HEADS
FAR = 1e30

W_SCALE = 32.0
UP_SCALE = 16.0


def alibi_slopes():
    s = 2.0 ** (-8.0 * np.arange(1, N_ALIBI + 1) / N_ALIBI)
    return s[B_HEADS:], s[:B_HEADS]


def penalty_tables(seq):
    slopes_a, slopes_b = alibi_slopes()
    rows = np.arange(P)[:, None]
    dist = np.abs(np.arange(2 * seq - P)[None, :] - (seq - P) - rows)
    times = sum(((dist % d == 0) & (dist <= w // 2)).astype(np.int64) for w, d in PATTERNS)
    log = np.log(np.maximum(times, 1))
    a = np.stack([np.where(times > 0, s * dist - log, FAR) for s in slopes_a], axis=1)
    near = np.abs(np.arange(3 * P)[None, :] - P - rows)
    b = np.stack([np.where(near <= B_WINDOW, s * near, FAR) for s in slopes_b], axis=1)
    return a.astype(np.float32), b.astype(np.float32)


def rope_frequencies():
    return (THETA ** (-2.0 * np.arange(HALF_ROPE) / ROPE)).astype(np.float32)


def encoder_kernel(nc, x, positions, pre_norm, w_in, q_a_norm, kv_a_norm, w_uq, w_ukv, sink, w_o, post_norm,
                   table_a, table_b, freq, eye, out):
    DEPTH, D, D_IN = w_in.shape
    SEQ = x.shape[1]
    TILES = SEQ // P
    KT = D // P
    SPAN = 2 * SEQ - P
    A_W, B_W, C_W = A_HEADS * HEAD, B_HEADS * HEAD, C_HEADS * HEAD
    assert SEQ == 1024 and D == 1024 and TILES == KT == 8

    CUTS = [0, 512, 1024, 1536, 2048, 2464, 2848]
    CHUNKS = 6
    assert CUTS[-1] == D_IN
    GATE = {1: (A_W, A_W, 0), 3: (2 * HEAD, B_W, A_W), 5: (0, C_W, A_W + B_W)}
    GROUPS = 8
    PROJ = CHUNKS * GROUPS

    PIECES = [("in", c, h) for c in range(CHUNKS) for h in range(2)] + [("up", 6, 0)]
    PIECES += [("out", c, h) for c in (7, 8) for h in range(2)]
    NP = len(PIECES)
    FIRST_PIECE = {c: min(i for i, p in enumerate(PIECES) if p[1] == c) for c in range(9)}
    UQ = C_HEADS * C_QK
    UKV = C_HEADS * 2 * HEAD
    UP_COLS = 2 * UQ + UKV

    UNITS = [("A", t, h) for t in range(TILES) for h in range(A_HEADS)]
    UNITS += [("B", t, h) for t in range(TILES) for h in range(B_HEADS)]
    UNITS += [("C", t, h) for t in range(TILES) for h in range(C_HEADS)]
    NU = len(UNITS)
    FROM = {"A": 0, "B": TILES * A_HEADS, "C": TILES * (A_HEADS + B_HEADS)}
    UPTO = {"A": FROM["B"], "B": FROM["C"], "C": NU}

    def key_tiles(u):
        branch, t, _ = UNITS[u]
        return range(max(t - 1, 0), min(t + 2, TILES)) if branch == "B" else range(TILES)

    HALVES = []
    HALF_FROM = []
    for u in range(NU):
        HALF_FROM.append(len(HALVES))
        tiles = list(key_tiles(u))
        HALVES += [(u, n, tiles[4 * n:4 * n + 4]) for n in range((len(tiles) + 3) // 4)]
    HALF_FROM.append(len(HALVES))
    NH = len(HALVES)

    def heads_of(u):
        return A_HEADS if UNITS[u][0] == "A" else GROUP

    OUT_GROUPS = []
    u = 0
    while u < NU:
        OUT_GROUPS.append((u, heads_of(u)))
        u += heads_of(u)
    NG = len(OUT_GROUPS)
    GROUP_OF = {u + i: g for g, (u, n) in enumerate(OUT_GROUPS) for i in range(n)}
    B_GROUPS = [g for g, (u, n) in enumerate(OUT_GROUPS) if UNITS[u][0] == "B"]
    SPLITS = [4, 12, 20, 28]
    FILL = CHUNKS - 2
    SPREAD = (UPTO["B"] - FROM["B"]) // (2 * GROUPS)
    assert SPREAD == GROUP == 3
    SPREAD_FROM = TILES + 2
    KV_STEPS = 3 * 2 + TILES

    with ExitStack() as ctx:
        def sb(name, cols, dt=F32):
            return ctx.enter_context(nc.sbuf_tensor(name, [P, cols], dt))

        def sem(name):
            return ctx.enter_context(nc.semaphore(name))

        hT = sb("hT", 2 * KT * SEQ, F16)
        hT_hi = hT[:, 0:KT * SEQ].rearrange("p (k s) -> p k s", k=KT)
        hT_lo = hT[:, KT * SEQ:].rearrange("p (k s) -> p k s", k=KT)
        y_sb = sb("y", TILES * D)
        y = y_sb[:, :].rearrange("p (t d) -> p t d", t=TILES)
        stage_sb = sb("stage", 2 * 2048)
        stage = [stage_sb[:, 2048 * i:2048 * (i + 1)] for i in range(2)]
        wbuf = [sb(f"w{i}", 2 * KT * 512, F16) for i in range(2)]
        w_hi_of = [w[:, 0:KT * 512] for w in wbuf]
        w_lo_of = [w[:, KT * 512:] for w in wbuf]
        z = sb("z", 32 * 1024 // 4 + A_HEADS * SPAN)
        pp = sb("pp", 4096)
        scratch = sb("scratch", 2 * UQ)
        g_pre = sb("g_pre", D)
        g_post = sb("g_post", D)
        g_lat = sb("g_lat", Q_LORA + KV_LORA)
        cos = sb("cos", TILES * HALF_ROPE)
        sin = sb("sin", TILES * HALF_ROPE)
        ident = sb("ident", P)
        sinks = sb("sinks", DEPTH * B_HEADS)
        sink_now = sb("sink_now", B_HEADS)
        neg_sink = sb("neg_sink", B_HEADS)
        low = sb("low", NU)
        mass = sb("mass", NU)
        shift = sb("shift", GROUP * 2)
        sunk = sb("sunk", GROUP * 2)
        total = sb("total", 2 * 4)
        inverse = sb("inverse", 2 * 4)
        stat = sb("stat", 8 * TILES)
        lat_stat = sb("lat_stat", 6 * TILES)
        eps_col = sb("eps_col", 1)

        zh = z[:, :].bitcast(F16)

        def zpart(start_bytes, shape, rows=P):
            n = int(np.prod(shape))
            v = zh[0:rows, start_bytes // 2:start_bytes // 2 + n]
            names = "abcd"[:len(shape)]
            return v.rearrange(f"p ({' '.join(names)}) -> p {' '.join(names)}",
                               **{k: s for k, s in zip(names[:-1], shape[:-1])})

        K1 = 1024
        q_a = zpart(0, [A_HEADS, SEQ])
        k_a = [zpart(8 * K1, [A_HEADS, SEQ]), zpart(16 * K1, [A_HEADS, SEQ])]
        v_a = zpart(24 * K1, [TILES, A_HEADS, 2 * HEAD])
        tab_a = z[:, 8192:8192 + A_HEADS * SPAN].rearrange("p (h s) -> p h s", h=A_HEADS)
        w_first = [zpart(24 * K1, [KT, 512]), zpart(32 * K1, [KT, 512])]
        q_b = zpart(0, [B_HEADS, SEQ])
        k_b = [zpart(12 * K1, [B_KV, SEQ]), zpart(16 * K1, [B_KV, SEQ])]
        v_b = zpart(20 * K1, [TILES, B_KV, 2 * HEAD])
        tab_b = z[:, 38 * K1 // 4:38 * K1 // 4 + B_HEADS * 3 * P].rearrange("p (h s) -> p h s", h=B_HEADS)
        q_c = [zpart(0, [C_HEADS, SEQ]), zpart(12 * K1, [C_HEADS, SEQ])]
        k_c = [zpart(24 * K1, [C_HEADS, SEQ]), zpart(36 * K1, [C_HEADS, SEQ])]
        v_c = zpart(48 * K1, [TILES, C_HEADS, 2 * HEAD])

        prob = [pp[:, 1024 * i:1024 * (i + 1)] for i in range(2)]
        prob_a = prob + [stage[0][:, 1024 * i:1024 * (i + 1)] for i in range(2)]
        prob_b = [pp[:, 3 * P * i:3 * P * (i + 1)] for i in range(4)]
        turned_b = [[pp[:, 2048 + 3 * P * i + 192 * j:2048 + 3 * P * i + 192 * (j + 1)].bitcast(F16)
                     .rearrange("p (b q) -> p b q", q=P) for j in range(2)] for i in range(4)]
        turned_sb = [[pp[:, 2048 + 1024 * i + 512 * j:2048 + 1024 * i + 512 * (j + 1)].bitcast(F16)
                      .rearrange("p (b q) -> p b q", q=P) for j in range(2)] for i in range(2)]
        xb = prob
        xn = [pp[:, 2048 + 1024 * i:2048 + 1024 * (i + 1)] for i in range(2)]
        LAT = Q_LORA + KV_LORA + ROPE
        lat_kv = [pp[:, 2048 * i + 1536:2048 * (i + 1)].bitcast(F16) for i in range(2)]
        lat_q = [zpart(52 * K1, [2, SEQ]), zpart(56 * K1, [2, SEQ])]
        lat_f = [z[:, 47 * K1 // 4 + LAT * i:47 * K1 // 4 + LAT * (i + 1)] for i in range(2)]
        lat_junk = z[:, 60 * K1 // 4:60 * K1 // 4 + Q_LORA + KV_LORA]
        EARLY_KV = 3 * 2 + 2
        assert 4 * A_HEADS * SPAN + 32 * K1 >= 60 * K1 + 4 * (Q_LORA + KV_LORA)
        assert 4 * B_HEADS * 3 * P <= 9 * K1
        qf = [scratch[:, UQ * i:UQ * (i + 1)].rearrange("p (h d) -> p h d", h=C_HEADS) for i in range(2)]
        o_tmp = [scratch[:, 256 * i:256 * (i + 1)] for i in range(2)]
        o_sum = [scratch[:, 512 + 256 * i:512 + 256 * (i + 1)] for i in range(2)]
        junk = scratch[:, 0:D]
        cos_v = cos[:, :].rearrange("p (t f) -> p t f", t=TILES)
        sin_v = sin[:, :].rearrange("p (t f) -> p t f", t=TILES)
        stat_v = stat[:, :].rearrange("p (k t) -> p k t", t=TILES)
        lat_stat_v = lat_stat[:, :].rearrange("p (k t c) -> p k t c", k=3, t=TILES)

        ps = ctx.enter_context(nc.psum_tensor("ps", [P, 8, 512], F32))

        def pair(b):
            return ps[:, b:b + 2, :]

        def x_banks(n):
            return 4 + 2 * (n % 2) if isinstance(n, int) and n < TILES - 1 else 4

        const_loaded = sem("const_loaded")
        piece_loaded = [sem("piece_loaded_even"), sem("piece_loaded_odd")]
        piece_hi, piece_lo = sem("piece_hi"), sem("piece_lo")
        gains_loaded, next_gain_loaded = sem("gains_loaded"), sem("next_gain_loaded")
        table_a_loaded, table_b_loaded = sem("table_a_loaded"), sem("table_b_loaded")
        first_x_loaded = [sem(f"first_x_loaded_{t}") for t in range(TILES)]
        x_copied = sem("x_copied")
        x_loaded = [sem("x_loaded_even"), sem("x_loaded_odd")]
        x_stored = [sem("x_stored_even"), sem("x_stored_odd")]
        rope_loaded = sem("rope_loaded")
        EACH = TILES // 2

        setup, carried = sem("setup"), sem("carried")
        angle, trig_step = sem("angle"), sem("trig_step")
        trig = sem("trig")
        pre_sq, pre_root, pre_inv = sem("pre_sq"), sem("pre_root"), sem("pre_inv")
        xn_done, x_turned, hT_hi_done, hT_done = sem("xn_done"), sem("x_turned"), sem("hT_hi_done"), sem("hT_done")
        proj_done, proj_act, proj_dve = sem("proj_done"), sem("proj_act"), sem("proj_dve")
        k_lo_done = sem("k_lo_done")
        gate_one, gate_inv = sem("gate_one"), sem("gate_inv")
        gains_scaled, sinks_negated = sem("gains_scaled"), sem("sinks_negated")
        lat_sq, lat_root, lat_inv = sem("lat_sq"), sem("lat_root"), sem("lat_inv")
        lat_prod, lat_done, lat_turned, lat_hi, lat_lo = (sem("lat_prod"), sem("lat_done"), sem("lat_turned"),
                                                         sem("lat_hi"), sem("lat_lo"))
        rope_spread = sem("rope_spread")
        kv_done, kv_hi, kv_lo = sem("kv_done"), sem("kv_hi"), sem("kv_lo")
        uq_done, uq_copied, uq_prod, uq_roped = sem("uq_done"), sem("uq_copied"), sem("uq_prod"), sem("uq_roped")
        uq_turned, uq_hi, uq_lo = sem("uq_turned"), sem("uq_hi"), sem("uq_lo")
        scores_done, low_done, exp_done = sem("scores_done"), sem("low_done"), sem("exp_done")
        prob_turned, prob_hi, prob_lo = sem("prob_turned"), sem("prob_hi"), sem("prob_lo")
        pv_done, o_copied, o_summed, y_gated, y_done = (sem("pv_done"), sem("o_copied"), sem("o_summed"),
                                                       sem("y_gated"), sem("y_done"))
        sink_shifted, sink_exp, sink_added, mass_inv = (sem("sink_shifted"), sem("sink_exp"), sem("sink_added"),
                                                       sem("mass_inv"))
        y_turned, yT_hi_done, yT_done = sem("y_turned"), sem("yT_hi_done"), sem("yT_done")
        out_done, post_sq, post_root, post_inv = sem("out_done"), sem("post_sq"), sem("post_root"), sem("post_inv")
        post_done, x_summed = sem("post_done"), sem("x_summed")

        block = ctx.enter_context(nc.Block())
        x_d = x.rearrange("b (t p) d -> (b t) p d", p=P)
        out_d = out.rearrange("b (t p) d -> (b t) p d", p=P)
        w_in_d = w_in.rearrange("l (k p) n -> l p k n", p=P)
        w_o_d = w_o.rearrange("l (k p) n -> l p k n", p=P)
        w_uq_d = w_uq.rearrange("l (k p) n -> l p k n", p=P)

        def bank_of(c, G):
            return G % 4 if c < FILL else 2 + G % 2

        def score_bank(u):
            return u % 2 if UNITS[u][0] == "B" else 2 * (u % 2)

        def depth(u):
            return 4 if UNITS[u][0] == "B" else 2

        def prob_of(u):
            return {"A": prob_a[u % 4], "B": prob_b[u % 4], "C": prob[u % 2]}[UNITS[u][0]]

        def turned_of(u):
            return turned_b[u % 4] if UNITS[u][0] == "B" else turned_sb[u % 2]

        def ahead(branch):
            return (3, 2) if branch == "B" else (2, 1)

        def groups_ending(u):
            return [g for g, (u0, n) in enumerate(OUT_GROUPS) if u0 + n - 1 == u]

        def early_scores(c):
            return {1: ("A", 1), 3: ("B", 2)}.get(c, ("", 0))

        EARLY = {"A": 1, "B": 2, "C": 1}

        def y_banks(t):
            return 6 if t else 2

        def y_groups(t):
            return GROUP_OF[FROM["C"] + C_HEADS * (t + 1) - 1] + 1

        def latent_bank(t):
            return 6 + (B_GROUPS[0] + t) % 2

        def one(t, L):
            return t[bass.ds(L, 1)]

        def piece_shape(i):
            kind, c, h = PIECES[i]
            cols = CUTS[c + 1] - CUTS[c] if kind == "in" else 512
            return kind, c, h, cols

        def staged(i):
            kind, c, h, cols = piece_shape(i)
            if kind == "up":
                return stage[i % 2][:, 0:UP_COLS]
            return stage[i % 2][:, 0:4 * cols].rearrange("p (k n) -> p k n", k=4)

        LOADS = [sum(3 if p[0] == "up" else 1 for p in PIECES[i::2]) for i in range(2)]

        def loads_upto(i):
            return sum(3 if p[0] == "up" else 1 for p in PIECES[i % 2:i + 1:2])

        def split_of(i, parts):
            kind, c, h, cols = piece_shape(i)
            if c == 0:
                return w_first[parts is w_lo_of][:, 4 * h:4 * h + 4, :]
            if kind == "up":
                return parts[c % 2][:, 0:UP_COLS]
            return parts[c % 2].rearrange("p (k n) -> p k n", k=KT)[:, 4 * h:4 * h + 4, 0:cols]

        def weights(c):
            if c == 0:
                return w_first
            return [w[c % 2].rearrange("p (k n) -> p k n", k=KT) for w in (w_hi_of, w_lo_of)]

        def carry(eng):
            eng.sem_inc(carried, 1)

        @block.sync
        def _(sp):
            sp.dma_start(low[:, 0:TILES].bitcast(I32), positions).then_inc(rope_loaded, 16)
            sp.dma_start(cos[:, :].rearrange("p (t f) -> p t f", t=TILES)[:, 0, :],
                         freq[0:1, :].broadcast_to([P, HALF_ROPE])).then_inc(rope_loaded, 16)
            for t in range(TILES):
                sp.dma_start(y[:, t, :], x_d[t]).then_inc(first_x_loaded[t], 16)
                if t == 0:
                    sp.dma_start(g_pre[:, :], pre_norm[0:1, :].broadcast_to([P, D])).then_inc(const_loaded, 16)
                    sp.dma_start(ident[:, :], eye).then_inc(const_loaded, 16)
            sp.dma_start(sinks[:, :], sink.rearrange("l h -> (l h)").unsqueeze(0)
                         .broadcast_to([P, DEPTH * B_HEADS])).then_inc(const_loaded, 16)
            def load_pieces(which, L, source):
                for i in which:
                    kind, c, h, cols = piece_shape(i)
                    n = L * NP + max(i, 1)
                    sp.wait_ge(piece_hi, n)
                    carry(sp)
                    sp.wait_ge(piece_lo, n)
                    carry(sp)
                    loaded = piece_loaded[i % 2]
                    if kind == "in":
                        sp.dma_start(staged(i), one(w_in_d, source)[0][:, 4 * h:4 * h + 4, CUTS[c]:CUTS[c + 1]]
                                     ).then_inc(loaded, 16)
                    elif kind == "out":
                        sp.dma_start(staged(i), one(w_o_d, source)[0][:, 4 * h:4 * h + 4, 512 * (c - 7):512 * (c - 6)]
                                     ).then_inc(loaded, 16)
                    else:
                        sp.dma_start(stage[i % 2][:, 0:2 * UQ].rearrange("p (k n) -> p k n", k=2),
                                     one(w_uq_d, source)[0]).then_inc(loaded, 16)
                        for part in range(2):
                            sp.dma_start(stage[i % 2][:, 2 * UQ + C_W * part:2 * UQ + C_W * (part + 1)]
                                         .rearrange("p (h d) -> p h d", d=HEAD),
                                         one(w_ukv, source)[0].rearrange("p (h c d) -> p c h d", c=2, d=HEAD)[:, part]
                                         ).then_inc(loaded, 16)

            def layer(L, is_last):
                sp.dma_start(g_lat[:, 0:Q_LORA], one(q_a_norm, L)[0].unsqueeze(0).broadcast_to([P, Q_LORA])
                             ).then_inc(gains_loaded, 16)
                sp.dma_start(g_lat[:, Q_LORA:], one(kv_a_norm, L)[0].unsqueeze(0).broadcast_to([P, KV_LORA])
                             ).then_inc(gains_loaded, 16)
                sp.dma_start(g_post[:, :], one(post_norm, L)[0].unsqueeze(0).broadcast_to([P, D])
                             ).then_inc(gains_loaded, 16)
                load_pieces(range(2, 6), L, L)
                sp.wait_ge(proj_done, L * PROJ + GROUPS)
                carry(sp)
                sp.dma_start(tab_a, table_a).then_inc(table_a_loaded, 16)
                sp.wait_ge(prob_turned, L * NH + HALF_FROM[UPTO["A"]])
                carry(sp)
                load_pieces(range(6, 8), L, L)
                sp.wait_ge(xn_done, TILES * L + TILES)
                carry(sp)
                sp.dma_start(g_pre[:, :], one(pre_norm[1:DEPTH + 1, :], L)[0].unsqueeze(0).broadcast_to([P, D])
                             ).then_inc(next_gain_loaded, 16)
                sp.wait_ge(low_done, L * NU + UPTO["A"])
                carry(sp)
                sp.wait_ge(pv_done, L * NU + UPTO["A"])
                carry(sp)
                sp.dma_start(tab_b, table_b).then_inc(table_b_loaded, 16)
                load_pieces(range(8, NP), L, L)
                load_pieces(range(2), L + 1, 0 if is_last else L + 1)
                sp.wait_ge(prob_turned, L * NH + NH)
                carry(sp)
                sp.wait_ge(pv_done, L * NU + NU)
                carry(sp)
                sp.wait_ge(x_copied, 16)
                carry(sp)
                for t in range(TILES):
                    if t >= 2:
                        sp.wait_ge(x_stored[t % 2], 16 * (EACH * L + t // 2))
                        carry(sp)
                        sp.wait_ge(xn_done, TILES * (L + 1) + t - 1)
                        carry(sp)
                    sp.dma_start(xb[t % 2], out_d[t]).then_inc(x_loaded[t % 2], 16)
                    if t >= 1:
                        sp.wait_ge(x_summed, TILES * L + t)
                        carry(sp)
                        sp.dma_start(out_d[t - 1], xb[(t - 1) % 2]).then_inc(x_stored[(t - 1) % 2], 16)
                sp.wait_ge(x_summed, TILES * L + TILES)
                carry(sp)
                sp.dma_start(out_d[TILES - 1], xb[(TILES - 1) % 2]).then_inc(x_stored[(TILES - 1) % 2], 16)
                for parity in range(2):
                    sp.wait_ge(x_stored[parity], 16 * EACH * (L + 1))
                    carry(sp)
                sp.wait_ge(xn_done, TILES * (L + 2))
                carry(sp)

            load_pieces(range(2), 0, 0)
            with sp.Fori(0, DEPTH - 1) as L:
                layer(L, False)
            layer(DEPTH - 1, True)
            for parity in range(2):
                sp.wait_ge(x_stored[parity], 16 * EACH * DEPTH)

        @block.gpsimd
        def _(pool):
            pool.wait_ge(proj_done, GROUPS)
            pool.dma_start(out_d, x_d).then_inc(x_copied, 16)
            with pool.Fori(0, DEPTH) as L:
                def gate(c, g):
                    frm, width, to = GATE[c]
                    pool.wait_ge(proj_act, L * PROJ + GROUPS * c + g + 1)
                    carry(pool)
                    nc.gpsimd.tensor_scalar(y[:, g, to:to + width], y[:, g, to:to + width], 1.0, None,
                                            ALU.add).then_inc(gate_one, 1)

                def spread_rope(part, heads):
                    for h in heads:
                        n = L * 2 * (C_HEADS - 1) + part * (C_HEADS - 1) + h
                        if h == 1:
                            pool.wait_ge(lat_lo, L * TILES + TILES)
                            carry(pool)
                            pool.wait_ge(low_done, L * NU + UPTO["A" if part == 0 else "B"])
                            carry(pool)
                        pool.wait_ge(y_done, L * NG + GROUP_OF[UPTO["B"] - 1] + 1 if part else
                                     L * NG + B_GROUPS[SPREAD_FROM] + h - 1)
                        carry(pool)
                        pool.wait_ge(gate_one, L * 3 * GROUPS + (3 * GROUPS if part else
                                                                 GROUPS + SPREAD_FROM + h))
                        carry(pool)
                        nc.gpsimd.tensor_copy(k_c[part][HEAD:C_QK, h, :], k_c[part][HEAD:C_QK, 0, :]
                                              ).then_inc(rope_spread, 1)
                        pool.wait_ge(rope_spread, n)
                        carry(pool)

                def branch(name, base):
                    for g, (u0, n) in enumerate(OUT_GROUPS):
                        if UNITS[u0][0] != name:
                            continue
                        if name == "B" and B_GROUPS.index(g) >= GROUPS:
                            gate(5, B_GROUPS.index(g) - GROUPS)
                        if name == "B" and SPREAD_FROM <= B_GROUPS.index(g) < SPREAD_FROM + C_HEADS - 1:
                            spread_rope(0, [B_GROUPS.index(g) - SPREAD_FROM + 1])
                        _, t, h0 = UNITS[u0]
                        cols = y[:, t, base + HEAD * h0:base + HEAD * (h0 + n)]
                        yv = cols.rearrange("p (h d) -> p h d", h=n)
                        pool.wait_ge(o_summed, L * NG + g + 1)
                        nc.gpsimd.tensor_tensor(cols, o_sum[g % 2][:, 0:HEAD * n], cols, ALU.mult
                                                ).then_inc(y_gated, 1)
                        pool.wait_ge(y_gated, L * NG + g + 1)
                        pool.wait_ge(mass_inv, L * NG + g + 1)
                        nc.gpsimd.tensor_tensor(yv, yv, inverse[:, 4 * (g % 2):4 * (g % 2) + n].unsqueeze(2)
                                                .broadcast_to([P, n, HEAD]), ALU.mult).then_inc(y_done, 1)

                for g in range(GROUPS):
                    gate(1, g)
                branch("A", 0)
                for g in range(GROUPS):
                    gate(3, g)
                branch("B", A_W)
                spread_rope(1, range(1, C_HEADS))
                branch("C", A_W + B_W)

        @block.scalar
        def _(act):
            act.wait_ge(setup, 1)
            nc.scalar.copy(eps_col[:, 0:1], eps_col[:, 0:1]).then_inc(piece_hi, 1)
            act.wait_ge(angle, 1)
            nc.scalar.activation(sin[:, :], low[:, 0:TILES * HALF_ROPE], ACT.Sin).then_inc(trig, 1)
            nc.scalar.activation(cos[:, :], mass[:, 0:TILES * HALF_ROPE], ACT.Sin).then_inc(trig, 1)
            act.wait_ge(piece_hi, 1)

            def square_norm(n, src, t):
                nc.scalar.activation(junk, src, ACT.Square, accum_out=stat_v[:, 0, t:t + 1]).then_inc(pre_sq, 1)
                act.wait_ge(pre_sq, n + 1)
                nc.scalar.activation(stat_v[:, 1, t:t + 1], stat_v[:, 0, t:t + 1], ACT.Sqrt, bias=eps_col[:, 0:1],
                                     scale=1.0 / D).then_inc(pre_root, 1)

            def high_of_h(n, t):
                act.wait_ge(x_turned, n + 1)
                nc.scalar.copy(hT_hi[:, :, P * t:P * (t + 1)], pair(x_banks(n)).rearrange("p b (k q) -> p (b k) q", q=P)
                               ).then_inc(hT_hi_done, 1)

            for t in range(TILES):
                act.wait_ge(first_x_loaded[t], 16)
                if t >= 1:
                    act.wait_ge(pre_sq, t)
                square_norm(t, y[:, t, :], t)
                if t >= 1:
                    high_of_h(t - 1, t - 1)
            act.wait_ge(trig, 2)

            def split(i, L):
                kind = PIECES[i][0]
                act.wait_ge(piece_loaded[i % 2], 16 * (L * LOADS[i % 2] + loads_upto(i)))
                nc.scalar.activation(split_of(i, w_hi_of), staged(i), ACT.Copy,
                                     scale=UP_SCALE if kind == "up" else W_SCALE).then_inc(piece_hi, 1)

            split(0, 0)
            split(1, 0)

            with act.Fori(0, DEPTH) as L:
                def project_group(c, g):
                    G = GROUPS * c + g
                    src = ps[:, bank_of(c, G), :]
                    act.wait_ge(proj_done, L * PROJ + G + 1)
                    if c in (0, 2):
                        s, j = divmod(g, 4)
                        tok = slice(512 * s, 512 * s + 512)
                        queries = j < (2 if c == 0 else 3)
                        for e in range(2):
                            if queries:
                                dst = (q_a if c == 0 else q_b)[0:HEAD, 2 * j + e, tok]
                                scale = -(HEAD ** -0.5) / W_SCALE
                            else:
                                dst = (k_a if c == 0 else k_b)[0][0:HEAD, 2 * (j % 2) * (c == 0) + e, tok]
                                scale = 1.0 / W_SCALE
                            last = nc.scalar.activation(dst, src[HEAD * e:HEAD * (e + 1), :], ACT.Copy,
                                                        scale=scale)
                        last.then_inc(proj_act, 1)
                    elif c == 4:
                        for k, (a, b) in enumerate(((0, Q_LORA), (Q_LORA, Q_LORA + KV_LORA))):
                            if k == 1 or g >= 1:
                                act.wait_ge(lat_sq, L * 2 * TILES + 2 * g + k)
                            last = nc.scalar.activation(lat_junk[:, a:b], src[:, a:b], ACT.Square,
                                                        scale=1.0 / (W_SCALE * math.sqrt(b - a)),
                                                        accum_out=lat_stat_v[:, 0, g, k:k + 1])
                            last.then_inc(lat_sq, 1)
                        act.wait_ge(lat_sq, L * 2 * TILES + 2 * g + 2)
                        nc.scalar.activation(lat_stat_v[:, 1, g, :], lat_stat_v[:, 0, g, :], ACT.Sqrt,
                                             bias=eps_col[:, 0:1]).then_inc(proj_act, 1)
                    else:
                        frm, width, to = GATE[c]
                        if c != 5:
                            dst = (v_a if c == 1 else v_b)[:, g, :, 0:HEAD]
                            nc.scalar.activation(dst, src[:, 0:frm].rearrange("p (h d) -> p h d", d=HEAD),
                                                 ACT.Copy, scale=1.0 / W_SCALE)
                        nc.scalar.activation(y[:, g, to:to + width], src[:, frm:frm + width], ACT.Exp,
                                             scale=-1.0 / W_SCALE).then_inc(proj_act, 1)
                    if c < FILL and g in (2, 5):
                        split(FIRST_PIECE[c + 1] + (g == 5), L)

                def project(c):
                    for g in range(GROUPS):
                        project_group(c, g)
                        if c == 0 and g == 0:
                            high_of_h(TILES * L + TILES - 1, TILES - 1)

                def latents_high(t):
                    act.wait_ge(lat_turned, L * TILES + t + 1)
                    tok = slice(P * t, P * (t + 1))
                    src = ps[:, latent_bank(t), :].rearrange("p (k q) -> p k q", q=P)
                    nc.scalar.copy(lat_q[0][:, :, tok], src[:, 0:2, :])
                    nc.scalar.copy(lat_kv[0][:, tok], src[:, 2, :])
                    nc.scalar.copy(k_c[0][HEAD:C_QK, 0, tok], src[0:ROPE, 3, :]).then_inc(lat_hi, 1)

                def up():
                    def keys_values(m):
                        src = ps[:, 6 + m % 2, :]
                        act.wait_ge(kv_done, L * KV_STEPS + m + 1)
                        if m < 6:
                            for e in range(2):
                                last = nc.scalar.activation(
                                    k_c[0][0:HEAD, 2 * (m // 2) + e, 512 * (m % 2):512 * (m % 2 + 1)],
                                    src[HEAD * e:HEAD * (e + 1), :], ACT.Copy, scale=1.0 / UP_SCALE)
                        else:
                            last = nc.scalar.activation(v_c[:, m - 6, :, 0:HEAD],
                                                        src[:, 0:C_W].rearrange("p (h d) -> p h d", d=HEAD),
                                                        ACT.Copy, scale=1.0 / UP_SCALE)
                        last.then_inc(kv_hi, 1)

                    def high_of_q(t):
                        act.wait_ge(uq_turned, L * TILES + t + 1)
                        src = pair(4).rearrange("p b (k q) -> p (b k) q", q=P)
                        nc.scalar.copy(q_c[0][0:C_QK, :, P * t:P * (t + 1)], src[0:C_QK, 0:C_HEADS, :]
                                       ).then_inc(uq_hi, 1)

                    for t in range(TILES):
                        act.wait_ge(uq_done, L * TILES + t + 1)
                        if t == 0:
                            act.wait_ge(y_gated, L * NG + GROUP_OF[UPTO["B"] - 1] + 1)
                        if t >= 2:
                            act.wait_ge(uq_turned, L * TILES + t - 1)
                        nc.scalar.activation(qf[t % 2].rearrange("p (b h) d -> p b (h d)", b=2),
                                             pair(2 * (t % 2))[:, :, 0:UQ // 2], ACT.Copy,
                                             scale=-(C_QK ** -0.5) / UP_SCALE).then_inc(uq_copied, 1)
                        keys_values(t)
                        if t >= 1:
                            high_of_q(t - 1)
                    keys_values(EARLY_KV)
                    high_of_q(TILES - 1)
                    for m in range(EARLY_KV + 1, KV_STEPS - 2):
                        keys_values(m)
                    exponentials(FROM["C"])
                    for m in range(KV_STEPS - 2, KV_STEPS):
                        keys_values(m)

                def exponentials(u):
                    branch = UNITS[u][0]
                    w = P * len(key_tiles(u))
                    act.wait_ge(low_done, L * NU + u + 1)
                    if branch == "C":
                        act.wait_ge(prob_turned, L * NH + HALF_FROM[u - 1])
                        src = pair(score_bank(u)).rearrange("p b n -> p (b n)")
                    else:
                        src = prob_of(u)[:, 0:w]
                    nc.scalar.activation(prob_of(u)[:, 0:w], src, ACT.Exp, scale=-1.0, bias=low[:, u:u + 1],
                                         accum_out=mass[:, u:u + 1]).then_inc(exp_done, 1)

                def high_of_prob(u):
                    for k in range(HALF_FROM[u], HALF_FROM[u + 1]):
                        _, half, tiles = HALVES[k]
                        act.wait_ge(prob_turned, L * NH + k + 1)
                        if half == 0 and u - depth(u) >= FROM[UNITS[u][0]]:
                            act.wait_ge(pv_done, L * NU + u - depth(u) + 1)
                        n = len(tiles)
                        nc.scalar.copy(turned_of(u)[0][:, 4 * half:4 * half + n, :],
                                       ps[:, 4 + k % 2, 0:P * n].rearrange("p (b q) -> p b q", q=P)
                                       ).then_inc(prob_hi, 1)

                def group_out(g):
                    u0, n = OUT_GROUPS[g]
                    if g in B_GROUPS:
                        i = B_GROUPS.index(g)
                        act.wait_ge(sink_shifted, L * len(B_GROUPS) + i + 1)
                        nc.scalar.activation(sunk[:, GROUP * (g % 2):GROUP * (g % 2 + 1)],
                                             shift[:, GROUP * (g % 2):GROUP * (g % 2 + 1)], ACT.Exp
                                             ).then_inc(sink_exp, 1)
                    act.wait_ge(pv_done, L * NU + u0 + n)
                    if g >= 2:
                        act.wait_ge(o_summed, L * NG + g - 1)
                    nc.scalar.copy(o_tmp[g % 2][:, 0:HEAD * n].rearrange("p (h d) -> p h d", h=n),
                                   ps[:, 6 + g % 2, 0:P * n].rearrange("p (h d) -> p h d", h=n)[:, :, HEAD:]
                                   ).then_inc(o_copied, 1)

                def between_b(i):
                    n, at = divmod(i, SPREAD)
                    if at == 0 and 2 <= n < TILES + 2:
                        latents_high(n - 2)
                    if at == 0 and 1 <= n <= 2 * GROUPS:
                        project_group(FILL + (n - 1) // GROUPS, (n - 1) % GROUPS)
                    if at == 1 and n >= 1:
                        split_after(n - 1)

                def split_after(n):
                    c, g = FILL + n // GROUPS, n % GROUPS
                    if c == FILL and g in (2, 5):
                        split(FIRST_PIECE[c + 1] + (g == 5), L)
                    if c == FILL + 1 and g == 2:
                        split(FIRST_PIECE[6], L)

                def high_of_y(t):
                    act.wait_ge(y_turned, L * TILES + t + 1)
                    nc.scalar.activation(hT_hi[:, :, P * t:P * (t + 1)],
                                         pair(y_banks(t)).rearrange("p b (k q) -> p (b k) q", q=P), ACT.Copy,
                                         scale=1.0 / W_SCALE).then_inc(yT_hi_done, 1)

                def attend(branch):
                    first, last = FROM[branch], UPTO[branch]
                    before, behind = ahead(branch)
                    for u in range(first + (branch == "C"), first + before - 1):
                        exponentials(u)
                    for i in range(first, last):
                        if branch != "A":
                            high_of_prob(i)
                        if i + before - 1 < last:
                            exponentials(i + before - 1)
                        if branch == "A":
                            high_of_prob(i)
                        if branch == "C" and i - first in SPLITS:
                            split(FIRST_PIECE[7] + SPLITS.index(i - first), L)
                        if branch == "B":
                            between_b(i - first)
                        if i - behind - 1 >= first:
                            for g in groups_ending(i - behind - 1):
                                group_out(g)
                    if branch == "B":
                        for i in range(last, last + SPREAD):
                            between_b(i - first)
                    if branch == "C":
                        high_of_y(0)
                    for u in range(last - behind - 1, last):
                        for g in groups_ending(u):
                            group_out(g)

                def finish():
                    for t in range(TILES):
                        if t + 1 < TILES:
                            high_of_y(t + 1)
                        act.wait_ge(out_done, L * TILES + t + 1)
                        if t == 0:
                            act.wait_ge(y_gated, L * NG + NG)
                        act.wait_ge(pre_sq, TILES * (L + 1) + t)
                        nc.scalar.activation(junk.rearrange("p (b n) -> p b n", b=2), pair(2 * (t % 2)), ACT.Square,
                                             scale=1.0 / W_SCALE, accum_out=stat_v[:, 3, t:t + 1]
                                             ).then_inc(post_sq, 1)
                        act.wait_ge(post_sq, L * TILES + t + 1)
                        nc.scalar.activation(stat_v[:, 4, t:t + 1], stat_v[:, 3, t:t + 1], ACT.Sqrt,
                                             bias=eps_col[:, 0:1], scale=1.0 / D).then_inc(post_root, 1)
                        if t >= 1:
                            high_of_h(TILES * (L + 1) + t - 1, t - 1)
                        act.wait_ge(x_summed, TILES * L + t + 1)
                        square_norm(TILES * (L + 1) + t, xb[t % 2], t)
                        if t in (2, 4):
                            split(t // 2 - 1, L + 1)

                project(0)
                project(1)
                attend("A")
                project(2)
                project(3)
                attend("B")
                up()
                attend("C")
                finish()

        @block.vector
        def _(dve):
            nc.vector.memset(eps_col[:, :], EPS).then_inc(setup, 1)

            def normalise(n, src, t):
                dve.wait_ge(pre_root, n + 1)
                nc.vector.reciprocal(stat_v[:, 2, t:t + 1], stat_v[:, 1, t:t + 1]).then_inc(pre_inv, 1)
                dve.wait_ge(pre_inv, n + 1)
                if not isinstance(n, int) or n >= 2:
                    dve.wait_ge(x_turned, n - 1)
                nc.vector.scalar_tensor_tensor(out=xn[t % 2], in0=src, scalar=stat_v[:, 2, t:t + 1], in1=g_pre[:, :],
                                               op0=ALU.mult, op1=ALU.mult).then_inc(xn_done, 1)

            def low_of_h(n, t):
                dve.wait_ge(hT_hi_done, n + 1)
                nc.vector.tensor_tensor(hT_lo[:, :, P * t:P * (t + 1)],
                                        pair(x_banks(n)).rearrange("p b (k q) -> p (b k) q", q=P),
                                        hT_hi[:, :, P * t:P * (t + 1)], ALU.subtract).then_inc(hT_done, 1)

            nc.vector.memset(sunk[:, :], 0.0).then_inc(piece_lo, 1)
            step = [0]

            def then(ins):
                step[0] += 1
                ins.then_inc(trig_step, 1)
                dve.wait_ge(trig_step, step[0])

            dve.wait_ge(rope_loaded, 16 * 2)
            R = TILES * HALF_ROPE
            posf = stat[:, 0:TILES]
            then(nc.vector.tensor_copy(posf, low[:, 0:TILES].bitcast(I32)))
            ang, turns, rest = (pp[:, R * i:R * (i + 1)] for i in range(3))
            then(nc.vector.tensor_tensor(ang.rearrange("p (t f) -> p t f", t=TILES),
                                         posf.unsqueeze(2).broadcast_to([P, TILES, HALF_ROPE]),
                                         cos_v[:, 0:1, :].broadcast_to([P, TILES, HALF_ROPE]), ALU.mult))
            ROUND = 1.5 * 2.0 ** 23
            PARTS = []
            left = 2.0 * math.pi
            for bits in (9, 12):
                e = 2.0 ** (bits - 1 - math.floor(math.log2(left)))
                PARTS.append(math.floor(left * e) / e)
                left -= PARTS[-1]
            PARTS.append(float(np.float32(left)))
            for target, quarter in ((low, 0.0), (mass, 0.25)):
                then(nc.vector.tensor_scalar(turns, ang, 1.0 / (2.0 * math.pi), quarter, ALU.mult, ALU.add))
                then(nc.vector.tensor_scalar(turns, turns, ROUND, None, ALU.add))
                then(nc.vector.tensor_scalar(turns, turns, ROUND, None, ALU.subtract))
                src = ang
                for part in PARTS:
                    then(nc.vector.scalar_tensor_tensor(out=rest, in0=turns, scalar=-part, in1=src,
                                                        op0=ALU.mult, op1=ALU.add))
                    src = rest
                if quarter:
                    then(nc.vector.tensor_scalar(rest, rest, math.pi / 2, None, ALU.add))
                then(nc.vector.tensor_scalar(target[:, 0:R], rest, 3.1415925, -3.1415925, ALU.min, ALU.max))
            nc.vector.memset(shift[:, :], 0.0).then_inc(angle, 1)

            dve.wait_ge(const_loaded, 16 * 3)
            for t in range(TILES):
                normalise(t, y[:, t, :], t)
                if t >= 1:
                    low_of_h(t - 1, t - 1)

            def split(i, L):
                kind = PIECES[i][0]
                dve.wait_ge(piece_hi, L * NP + i + 2)
                nc.vector.scalar_tensor_tensor(out=split_of(i, w_lo_of), in0=staged(i),
                                               scalar=UP_SCALE if kind == "up" else W_SCALE,
                                               in1=split_of(i, w_hi_of), op0=ALU.mult, op1=ALU.subtract
                                               ).then_inc(piece_lo, 1)

            split(0, 0)
            split(1, 0)

            with dve.Fori(0, DEPTH) as L:
                def low_part(dst, src, scale, high):
                    return nc.vector.scalar_tensor_tensor(out=dst, in0=src, scalar=scale, in1=high, op0=ALU.mult,
                                                          op1=ALU.subtract)

                def project_group(c, g):
                    G = GROUPS * c + g
                    src = ps[:, bank_of(c, G), :]
                    dve.wait_ge(proj_act, L * PROJ + G + 1)
                    if c in (0, 2):
                        s, j = divmod(g, 4)
                        tok = slice(512 * s, 512 * s + 512)
                        if j < (2 if c == 0 else 3):
                            q = q_a if c == 0 else q_b
                            for e in range(2):
                                last = low_part(q[HEAD:P, 2 * j + e, tok], src[HEAD * e:HEAD * (e + 1), :],
                                                -(HEAD ** -0.5) / W_SCALE, q[0:HEAD, 2 * j + e, tok])
                            last.then_inc(proj_dve, 1)
                        else:
                            ks = k_a if c == 0 else k_b
                            h0 = 2 * (j % 2) * (c == 0)
                            for e in range(2):
                                last = low_part(ks[1][0:HEAD, h0 + e, tok], src[HEAD * e:HEAD * (e + 1), :],
                                                1.0 / W_SCALE, ks[0][0:HEAD, h0 + e, tok])
                            last.then_inc(k_lo_done, 1)
                            nc.vector.tensor_copy(ks[0][HEAD:P, h0:h0 + 2, tok], ks[0][0:HEAD, h0:h0 + 2, tok])
                            dve.wait_ge(k_lo_done, L * 6 + (2 * s + j - 1 if c == 0 else 5 + s))
                            nc.vector.tensor_copy(ks[1][HEAD:P, h0:h0 + 2, tok], ks[1][0:HEAD, h0:h0 + 2, tok]
                                                  ).then_inc(proj_dve, 1)
                    elif c == 4:
                        t = g
                        nc.vector.reciprocal(lat_stat_v[:, 2, t, :], lat_stat_v[:, 1, t, :]).then_inc(lat_inv, 1)
                        f = lat_f[t % 2]
                        tmp = scratch[:, D:D + 4 * HALF_ROPE].rearrange("p (k f) -> p k f", k=4)
                        if t >= 2:
                            dve.wait_ge(lat_turned, L * TILES + t - 1)
                        if t >= 1:
                            dve.wait_ge(lat_done, L * TILES + t)
                        a, b = Q_LORA + KV_LORA, Q_LORA + KV_LORA + HALF_ROPE
                        for k, (col, table) in enumerate(((a, cos_v), (b, sin_v), (a, sin_v), (b, cos_v))):
                            last = nc.vector.scalar_tensor_tensor(
                                out=tmp[:, k, :], in0=src[:, col:col + HALF_ROPE], scalar=1.0 / W_SCALE,
                                in1=table[:, t, :], op0=ALU.mult, op1=ALU.mult)
                        last.then_inc(lat_prod, 1)
                        dve.wait_ge(lat_inv, L * TILES + t + 1)
                        for k, (p, q) in enumerate(((0, Q_LORA), (Q_LORA, a))):
                            last = nc.vector.scalar_tensor_tensor(
                                out=f[:, p:q], in0=src[:, p:q], scalar=lat_stat_v[:, 2, t, k:k + 1],
                                in1=g_lat[:, p:q], op0=ALU.mult, op1=ALU.mult)
                        last.then_inc(proj_dve, 1)
                        dve.wait_ge(lat_prod, L * TILES + t + 1)
                        nc.vector.tensor_tensor(f[:, a:b], tmp[:, 0, :], tmp[:, 1, :], ALU.subtract)
                        nc.vector.tensor_tensor(f[:, b:b + HALF_ROPE], tmp[:, 2, :], tmp[:, 3, :], ALU.add
                                                ).then_inc(lat_done, 1)
                    else:
                        frm, width, to = GATE[c]
                        if c != 5:
                            v = v_a if c == 1 else v_b
                            low_part(v[:, g, :, HEAD:], src[:, 0:frm].rearrange("p (h d) -> p h d", d=HEAD),
                                     1.0 / W_SCALE, v[:, g, :, 0:HEAD])
                        n = GROUPS * (c // 2) + g + 1
                        gate = y[:, g, to:to + width]
                        dve.wait_ge(gate_one, L * 3 * GROUPS + n)
                        nc.vector.reciprocal(gate, gate).then_inc(gate_inv, 1)
                        dve.wait_ge(gate_inv, L * 3 * GROUPS + n)
                        nc.vector.tensor_tensor(gate, src[:, frm:frm + width], gate, ALU.mult
                                                ).then_inc(proj_dve, 1)
                    if c < FILL and g in (2, 5):
                        split(FIRST_PIECE[c + 1] + (g == 5), L)

                def project(c):
                    for g in range(GROUPS):
                        if g == GROUPS - 1:
                            branch, early = early_scores(c)
                            if c == 1:
                                dve.wait_ge(table_a_loaded, 16 * (L + 1))
                            if c == 3:
                                dve.wait_ge(table_b_loaded, 16 * (L + 1))
                            for u in range(early):
                                lowest(FROM[branch] + u)
                        project_group(c, g)
                        if c == 0 and g == 0:
                            low_of_h(TILES * L + TILES - 1, TILES - 1)

                def latents_low(t):
                    dve.wait_ge(lat_hi, L * TILES + t + 1)
                    tok = slice(P * t, P * (t + 1))
                    src = ps[:, latent_bank(t), :].rearrange("p (k q) -> p k q", q=P)
                    nc.vector.tensor_tensor(lat_q[1][:, :, tok], src[:, 0:2, :], lat_q[0][:, :, tok], ALU.subtract)
                    nc.vector.tensor_tensor(lat_kv[1][:, tok], src[:, 2, :], lat_kv[0][:, tok], ALU.subtract)
                    nc.vector.tensor_tensor(k_c[1][HEAD:C_QK, 0, tok], src[0:ROPE, 3, :],
                                            k_c[0][HEAD:C_QK, 0, tok], ALU.subtract).then_inc(lat_lo, 1)

                def up():
                    def keys_values(m):
                        src = ps[:, 6 + m % 2, :]
                        dve.wait_ge(kv_hi, L * KV_STEPS + m + 1)
                        if m < 6:
                            tok = slice(512 * (m % 2), 512 * (m % 2 + 1))
                            for e in range(2):
                                h = 2 * (m // 2) + e
                                last = low_part(k_c[1][0:HEAD, h, tok], src[HEAD * e:HEAD * (e + 1), :],
                                                1.0 / UP_SCALE, k_c[0][0:HEAD, h, tok])
                        else:
                            last = low_part(v_c[:, m - 6, :, HEAD:],
                                            src[:, 0:C_W].rearrange("p (h d) -> p h d", d=HEAD), 1.0 / UP_SCALE,
                                            v_c[:, m - 6, :, 0:HEAD])
                        last.then_inc(kv_lo, 1)

                    def low_of_q(t):
                        dve.wait_ge(uq_hi, L * TILES + t + 1)
                        src = pair(4).rearrange("p b (k q) -> p (b k) q", q=P)
                        tok = slice(P * t, P * (t + 1))
                        nc.vector.tensor_tensor(q_c[1][0:C_QK, :, tok], src[0:C_QK, 0:C_HEADS, :],
                                                q_c[0][0:C_QK, :, tok], ALU.subtract).then_inc(uq_lo, 1)

                    for t in range(TILES):
                        f = qf[t % 2]
                        t1, t2 = f[:, :, HEAD:HEAD + HALF_ROPE], f[:, :, HEAD + HALF_ROPE:C_QK]
                        tmp = pp[:, 3072:3072 + 4 * C_HEADS * HALF_ROPE].rearrange("p (k h f) -> p k h f", k=4,
                                                                                   f=HALF_ROPE)
                        c_t = cos_v[:, t:t + 1, :].broadcast_to([P, C_HEADS, HALF_ROPE])
                        s_t = sin_v[:, t:t + 1, :].broadcast_to([P, C_HEADS, HALF_ROPE])
                        dve.wait_ge(uq_copied, L * TILES + t + 1)
                        if t >= 1:
                            dve.wait_ge(uq_roped, L * TILES + t)
                        for k, (part, table) in enumerate(((t1, c_t), (t2, s_t), (t1, s_t), (t2, c_t))):
                            last = nc.vector.tensor_tensor(tmp[:, k, :, :], part, table, ALU.mult)
                        last.then_inc(uq_prod, 1)
                        dve.wait_ge(uq_prod, L * TILES + t + 1)
                        nc.vector.tensor_tensor(t1, tmp[:, 0, :, :], tmp[:, 1, :, :], ALU.subtract)
                        nc.vector.tensor_tensor(t2, tmp[:, 2, :, :], tmp[:, 3, :, :], ALU.add).then_inc(uq_roped, 1)
                        keys_values(t)
                        if t >= 1:
                            low_of_q(t - 1)
                    keys_values(EARLY_KV)
                    low_of_q(TILES - 1)
                    keys_values(EARLY_KV + 1)
                    lowest(FROM["C"])
                    for m in range(EARLY_KV + 2, KV_STEPS):
                        keys_values(m)

                def lowest(u):
                    branch, t, h = UNITS[u]
                    tiles = key_tiles(u)
                    w = P * len(tiles)
                    dve.wait_ge(scores_done, L * NU + u + 1)
                    src = pair(score_bank(u)).rearrange("p b n -> p (b n)")[:, 0:w]
                    if branch == "C":
                        nc.vector.tensor_reduce(low[:, u:u + 1], src, AXES.X, ALU.min).then_inc(low_done, 1)
                        return
                    if u - 4 >= FROM[branch]:
                        dve.wait_ge(prob_turned, L * NH + HALF_FROM[u - 3])
                    if branch == "A":
                        at = SEQ - P - P * t
                        table, first = tab_a[:, h, at:at + w], FAR
                    else:
                        at = P * (tiles[0] - t + 1)
                        table, first = tab_b[:, h, at:at + w], neg_sink[:, h:h + 1]
                    carry(dve)
                    nc.vector.tensor_tensor_reduce(out=prob_of(u)[:, 0:w], in0=src, in1=table, scale=1.0,
                                                   scalar=first, op0=ALU.add, op1=ALU.min,
                                                   accum_out=low[:, u:u + 1]).then_inc(low_done, 1)

                def low_of_prob(u):
                    for k in range(HALF_FROM[u], HALF_FROM[u + 1]):
                        _, half, tiles = HALVES[k]
                        n = len(tiles)
                        dve.wait_ge(prob_hi, L * NH + k + 1)
                        nc.vector.tensor_tensor(turned_of(u)[1][:, 4 * half:4 * half + n, :],
                                                ps[:, 4 + k % 2, 0:P * n].rearrange("p (b q) -> p b q", q=P),
                                                turned_of(u)[0][:, 4 * half:4 * half + n, :], ALU.subtract
                                                ).then_inc(prob_lo, 1)

                def group_mass(g):
                    u0, n = OUT_GROUPS[g]
                    dst = inverse[:, 4 * (g % 2):4 * (g % 2) + n]
                    dve.wait_ge(exp_done, L * NU + u0 + n)
                    if g >= 2:
                        dve.wait_ge(y_done, L * NG + g - 1)
                    if g in B_GROUPS:
                        i = B_GROUPS.index(g)
                        h0 = UNITS[u0][2]
                        at = slice(GROUP * (g % 2), GROUP * (g % 2 + 1))
                        nc.vector.tensor_tensor(shift[:, at], low[:, u0:u0 + n], sink_now[:, h0:h0 + n], ALU.add
                                                ).then_inc(sink_shifted, 1)
                        dve.wait_ge(sink_exp, L * len(B_GROUPS) + i + 1)
                        nc.vector.tensor_tensor(total[:, 4 * (g % 2):4 * (g % 2) + n], mass[:, u0:u0 + n],
                                                sunk[:, at], ALU.add).then_inc(sink_added, 1)
                        dve.wait_ge(sink_added, L * len(B_GROUPS) + i + 1)
                        nc.vector.reciprocal(dst, total[:, 4 * (g % 2):4 * (g % 2) + n]).then_inc(mass_inv, 1)
                    else:
                        nc.vector.reciprocal(dst, mass[:, u0:u0 + n]).then_inc(mass_inv, 1)

                def group_out(g):
                    u0, n = OUT_GROUPS[g]
                    group_mass(g)
                    dve.wait_ge(o_copied, L * NG + g + 1)
                    nc.vector.tensor_tensor(o_sum[g % 2][:, 0:HEAD * n].rearrange("p (h d) -> p h d", h=n),
                                            ps[:, 6 + g % 2, 0:P * n].rearrange("p (h d) -> p h d", h=n)[:, :, 0:HEAD],
                                            o_tmp[g % 2][:, 0:HEAD * n].rearrange("p (h d) -> p h d", h=n), ALU.add
                                            ).then_inc(o_summed, 1)

                def between_b(i):
                    n, at = divmod(i, SPREAD)
                    if at == 1 and 2 <= n < TILES + 2:
                        latents_low(n - 2)
                    if at == 1 and 1 <= n <= 2 * GROUPS:
                        project_group(FILL + (n - 1) // GROUPS, (n - 1) % GROUPS)
                    if at == 0 and n >= 2:
                        split_after(n - 2)

                def split_after(n):
                    c, g = FILL + n // GROUPS, n % GROUPS
                    if c == FILL and g in (2, 5):
                        split(FIRST_PIECE[c + 1] + (g == 5), L)
                    if c == FILL + 1 and g == 2:
                        split(FIRST_PIECE[6], L)

                def low_of_y(t):
                    dve.wait_ge(yT_hi_done, L * TILES + t + 1)
                    low_part(hT_lo[:, :, P * t:P * (t + 1)], pair(y_banks(t)).rearrange("p b (k q) -> p (b k) q", q=P),
                             1.0 / W_SCALE, hT_hi[:, :, P * t:P * (t + 1)]).then_inc(yT_done, 1)

                def attend(branch):
                    first, last = FROM[branch], UPTO[branch]
                    before, behind = ahead(branch)
                    for u in range(first + EARLY[branch], first + before):
                        lowest(u)
                    for i in range(first, last):
                        if branch == "C":
                            low_of_prob(i)
                        if i + before < last:
                            lowest(i + before)
                        if branch != "C":
                            low_of_prob(i)
                        if branch == "C" and i - first in SPLITS:
                            split(FIRST_PIECE[7] + SPLITS.index(i - first), L)
                        if branch == "B":
                            between_b(i - first)
                        if i - behind - 1 >= first:
                            for g in groups_ending(i - behind - 1):
                                group_out(g)
                    if branch == "C":
                        low_of_y(0)
                    for u in range(last - behind - 1, last):
                        for g in groups_ending(u):
                            group_out(g)
                    if branch == "B":
                        for i in range(last, last + SPREAD):
                            between_b(i - first)

                def finish():
                    dve.wait_ge(next_gain_loaded, 16 * (L + 1))
                    for t in range(TILES):
                        if t + 1 < TILES:
                            low_of_y(t + 1)
                        dve.wait_ge(post_root, L * TILES + t + 1)
                        nc.vector.reciprocal(stat_v[:, 5, t:t + 1], stat_v[:, 4, t:t + 1]).then_inc(post_inv, 1)
                        dve.wait_ge(post_inv, L * TILES + t + 1)
                        if t == 0:
                            dve.wait_ge(pv_done, L * NU + NU)
                        else:
                            dve.wait_ge(x_turned, TILES * (L + 1) + t - 1)
                        nc.vector.scalar_tensor_tensor(out=xn[t % 2].rearrange("p (b n) -> p b n", b=2),
                                                       in0=pair(2 * (t % 2)), scalar=stat_v[:, 5, t:t + 1],
                                                       in1=g_post[:, :].rearrange("p (b n) -> p b n", b=2),
                                                       op0=ALU.mult, op1=ALU.mult).then_inc(post_done, 1)
                        dve.wait_ge(post_done, L * TILES + t + 1)
                        dve.wait_ge(x_loaded[t % 2], 16 * (EACH * L + t // 2 + 1))
                        nc.vector.tensor_tensor(xb[t % 2], xb[t % 2], xn[t % 2], ALU.add).then_inc(x_summed, 1)
                        if t >= 1:
                            low_of_h(TILES * (L + 1) + t - 1, t - 1)
                        dve.wait_ge(x_summed, TILES * L + t + 1)
                        normalise(TILES * (L + 1) + t, xb[t % 2], t)
                        if t in (2, 4):
                            split(t // 2 - 1, L + 1)

                dve.wait_ge(gains_loaded, 48 * (L + 1))
                nc.vector.tensor_scalar(g_lat[:, :], g_lat[:, :], 1.0 / W_SCALE, None, ALU.mult
                                        ).then_inc(gains_scaled, 1)
                nc.vector.tensor_scalar(g_post[:, :], g_post[:, :], 1.0 / W_SCALE, None, ALU.mult
                                        ).then_inc(gains_scaled, 1)
                now = sinks[:, :].rearrange("p (l h) -> p l h", h=B_HEADS)[:, bass.ds(L, 1), :]
                nc.vector.tensor_scalar(sink_now[:, :].unsqueeze(1), now, 1.0, None, ALU.mult).then_inc(sinks_negated, 1)
                nc.vector.tensor_scalar(neg_sink[:, :].unsqueeze(1), now, -1.0, None, ALU.mult
                                        ).then_inc(sinks_negated, 1)
                dve.wait_ge(gains_scaled, 2 * (L + 1))
                dve.wait_ge(sinks_negated, 2 * (L + 1))
                project(0)
                project(1)
                attend("A")
                project(2)
                project(3)
                attend("B")
                up()
                attend("C")
                finish()

        @block.tensor
        def _(pe):
            def turn_x(n, t):
                pe.wait_ge(xn_done, n + 1)
                if not isinstance(n, int):
                    pe.wait_ge(hT_done, n)
                elif n >= 2:
                    pe.wait_ge(hT_done, n - 1)
                for k in range(KT):
                    last = nc.tensor.transpose(ps[:, x_banks(n) + k // 4, P * (k % 4):P * (k % 4 + 1)],
                                               xn[t % 2][:, P * k:P * (k + 1)], ident[:, :])
                last.then_inc(x_turned, 1)

            pe.wait_ge(const_loaded, 16 * 3)
            for t in range(TILES - 1):
                turn_x(t, t)

            with pe.Fori(0, DEPTH) as L:
                def project_group(c, g, part=0, parts=1):
                    n = CUTS[c + 1] - CUTS[c]
                    hi, lo = weights(c)
                    G = GROUPS * c + g
                    held = 4 if c < FILL else 2
                    if part == 0:
                        if c == 0:
                            pe.wait_ge(hT_done, TILES * L + 4 * (g // 4) + 4)
                        if G in (2, 3):
                            pe.wait_ge(post_done, L * TILES)
                        if G >= 4:
                            pe.wait_ge(proj_act, L * PROJ + G - held + 1)
                            pe.wait_ge(proj_dve, L * PROJ + G - held + 1)
                    dst = ps[:, bank_of(c, G), 0:n]
                    products = [(k, m) for k in range(KT) for m in range(3)]
                    each = len(products) // parts
                    for k, m in products[each * part:each * (part + 1)]:
                        if g == 0 and k % 4 == 0 and m == 0:
                            pe.wait_ge(piece_lo, L * NP + FIRST_PIECE[c] + k // 4 + 2)
                        if c in (0, 2):
                            s, j = divmod(g, 4)
                            tok, cols = slice(512 * s, 512 * s + 512), slice(P * j, P * (j + 1))
                            a, b = ((hi[:, k, cols], hT_hi[:, k, tok]), (hi[:, k, cols], hT_lo[:, k, tok]),
                                    (lo[:, k, cols], hT_hi[:, k, tok]))[m]
                        else:
                            tok = slice(P * g, P * (g + 1))
                            a, b = ((hT_hi[:, k, tok], hi[:, k, 0:n]), (hT_hi[:, k, tok], lo[:, k, 0:n]),
                                    (hT_lo[:, k, tok], hi[:, k, 0:n]))[m]
                        last = nc.tensor.matmul(dst, a, b, start=(k == 0 and m == 0),
                                                stop=(k == KT - 1 and m == 2))
                    if part == parts - 1:
                        last.then_inc(proj_done, 1)

                def project(c, from_group=0):
                    for g in range(from_group, GROUPS):
                        if g == GROUPS - 1 and early_scores(c)[1]:
                            pe.wait_ge(proj_act, L * PROJ + GROUPS * c + g - 1)
                            pe.wait_ge(proj_dve, L * PROJ + GROUPS * c + g - 1)
                            branch, early = early_scores(c)
                            for u in range(early):
                                scores(FROM[branch] + u)
                        project_group(c, g)
                        if c == 0 and g == 0:
                            turn_x(TILES * L + TILES - 1, TILES - 1)

                def turn_latents(t):
                    pe.wait_ge(lat_done, L * TILES + t + 1)
                    pe.wait_ge(proj_dve, L * PROJ + GROUPS * 4 + t + 1)
                    pe.wait_ge(o_summed, L * NG + B_GROUPS[t] + 1)
                    for k in range(4):
                        w = ROPE if k == 3 else P
                        last = nc.tensor.transpose(ps[0:w, latent_bank(t), P * k:P * (k + 1)],
                                                   lat_f[t % 2][:, P * k:P * k + w], ident[:, :])
                    last.then_inc(lat_turned, 1)

                def three(dst, a, b, first, last):
                    for m, (p, q) in enumerate(((a[0], b[0]), (a[0], b[1]), (a[1], b[0]))):
                        ins = nc.tensor.matmul(dst, p, q, start=(first and m == 0), stop=(last and m == 2))
                    return ins

                def up():
                    wq = [w[0][:, 0:2 * UQ].rearrange("p (k n) -> p k n", k=2) for w in (w_hi_of, w_lo_of)]
                    wkv = [w[0][:, 2 * UQ:UP_COLS].rearrange("p (c n) -> p c n", c=2)
                           for w in (w_hi_of, w_lo_of)]
                    pe.wait_ge(piece_lo, L * NP + FIRST_PIECE[6] + 2)
                    pe.wait_ge(lat_lo, L * TILES + TILES)

                    def keys_values(m):
                        if m >= 2:
                            pe.wait_ge(kv_hi, L * KV_STEPS + m - 1)
                            pe.wait_ge(kv_lo, L * KV_STEPS + m - 1)
                        else:
                            pe.wait_ge(o_summed, L * NG + GROUP_OF[UPTO["B"] - 1] + m)
                        dst = ps[:, 6 + m % 2, :]
                        if m < 6:
                            h, s = m // 2, m % 2
                            ins = three(dst, [w[:, 0, P * h:P * (h + 1)] for w in wkv],
                                        [v[:, 512 * s:512 * (s + 1)] for v in lat_kv], True, True)
                        else:
                            t = m - 6
                            ins = three(dst[:, 0:C_W], [v[:, P * t:P * (t + 1)] for v in lat_kv],
                                        [w[:, 1, :] for w in wkv], True, True)
                        ins.then_inc(kv_done, 1)

                    def turn_q(t):
                        pe.wait_ge(uq_roped, L * TILES + t + 1)
                        if t >= 1:
                            pe.wait_ge(uq_lo, L * TILES + t)
                        else:
                            pe.wait_ge(prob_lo, L * NH + HALF_FROM[UPTO["B"]])
                        for h in range(C_HEADS):
                            last = nc.tensor.transpose(ps[0:C_QK, 4 + h // 4, P * (h % 4):P * (h % 4 + 1)],
                                                       qf[t % 2][:, h, :], ident[:, :])
                        last.then_inc(uq_turned, 1)

                    for t in range(TILES):
                        if t >= 2:
                            pe.wait_ge(uq_copied, L * TILES + t - 1)
                        elif t == 1:
                            pe.wait_ge(proj_act, L * PROJ + PROJ)
                            pe.wait_ge(proj_dve, L * PROJ + PROJ)
                        else:
                            pe.wait_ge(low_done, L * NU + UPTO["B"])
                        for b in range(2):
                            for k in range(2):
                                ins = three(ps[:, 2 * (t % 2) + b, 0:UQ // 2],
                                            [v[:, k, P * t:P * (t + 1)] for v in lat_q],
                                            [w[:, k, UQ // 2 * b:UQ // 2 * (b + 1)] for w in wq], k == 0, k == 1)
                        ins.then_inc(uq_done, 1)
                        keys_values(t)
                        if t >= 1:
                            turn_q(t - 1)
                    pe.wait_ge(uq_copied, L * TILES + TILES - 1)
                    pe.wait_ge(uq_lo, L * TILES + 1)
                    pe.wait_ge(kv_lo, L * KV_STEPS + 6)
                    pe.wait_ge(rope_spread, (L + 1) * 2 * (C_HEADS - 1))
                    keys_values(EARLY_KV)
                    scores(FROM["C"])
                    turn_q(TILES - 1)
                    for m in range(EARLY_KV + 1, KV_STEPS):
                        keys_values(m)

                def scores(u):
                    branch, t, h = UNITS[u]
                    tiles = key_tiles(u)
                    w = P * len(tiles)
                    if u - 2 >= FROM[branch]:
                        pe.wait_ge(exp_done if branch == "C" else low_done, L * NU + u - 1)
                    tok = slice(P * t, P * (t + 1))
                    for b in range((w + 511) // 512):
                        n = min(512, w - 512 * b)
                        keys = slice(P * tiles[0] + 512 * b, P * tiles[0] + 512 * b + n)
                        dst = ps[:, score_bank(u) + b, 0:n]
                        if branch == "C":
                            last = three(dst, [q[0:C_QK, h, tok] for q in q_c], [k[0:C_QK, h, keys] for k in k_c],
                                         True, True)
                        else:
                            q, ks, kh = (q_a, k_a, h) if branch == "A" else (q_b, k_b, h // GROUP)
                            for m in range(2):
                                last = nc.tensor.matmul(dst, q[:, h, tok], ks[m][:, kh, keys], start=(m == 0),
                                                        stop=(m == 1))
                    last.then_inc(scores_done, 1)

                def turn(u):
                    pe.wait_ge(exp_done, L * NU + u + 1)
                    for k in range(HALF_FROM[u], HALF_FROM[u + 1]):
                        _, half, tiles = HALVES[k]
                        if k >= 2:
                            pe.wait_ge(prob_lo, L * NH + k - 1)
                        for b in range(len(tiles)):
                            last = nc.tensor.transpose(ps[:, 4 + k % 2, P * b:P * (b + 1)],
                                                       prob_of(u)[:, 512 * half + P * b:512 * half + P * (b + 1)],
                                                       ident[:, :])
                        last.then_inc(prob_turned, 1)

                def values(u):
                    branch, t, h = UNITS[u]
                    g = GROUP_OF[u]
                    u0 = OUT_GROUPS[g][0]
                    v, vh = {"A": (v_a, h), "B": (v_b, h // GROUP), "C": (v_c, h)}[branch]
                    pe.wait_ge(prob_lo, L * NH + HALF_FROM[u + 1])
                    if u == u0 and g >= 2:
                        pe.wait_ge(o_summed, L * NG + g - 1)
                        t = B_GROUPS.index(g) - 2 if branch == "B" else -1
                        if 0 <= t < TILES:
                            pe.wait_ge(lat_lo, L * TILES + t + 1)
                    hi, lo = turned_of(u)
                    dst = ps[:, 6 + g % 2, P * (u - u0):P * (u - u0 + 1)]
                    tiles = key_tiles(u)
                    for b, kt in enumerate(tiles):
                        def high_terms():
                            return nc.tensor.matmul(dst, hi[:, b, :], v[:, kt, vh, :], start=(b == 0),
                                                    stop=(b == len(tiles) - 1), skip_group_check=True)

                        def low_term():
                            nc.tensor.matmul(dst[:, 0:HEAD], lo[:, b, :], v[:, kt, vh, 0:HEAD], start=False,
                                             stop=False, skip_group_check=True)

                        if b < len(tiles) - 1:
                            high_terms()
                            low_term()
                        else:
                            low_term()
                            last = high_terms()
                    last.then_inc(pv_done, 1)

                def attend(branch):
                    first, last = FROM[branch], UPTO[branch]
                    before, behind = ahead(branch)
                    turn(first)
                    if branch != "C":
                        chunk = 1 if branch == "A" else 3
                        pe.wait_ge(proj_act, L * PROJ + GROUPS * (chunk + 1))
                        pe.wait_ge(proj_dve, L * PROJ + GROUPS * (chunk + 1))
                    for u in range(first + EARLY[branch], first + before):
                        scores(u)
                    for i in range(first, last):
                        if i > first and branch != "A":
                            turn(i)
                        if i + before < last:
                            scores(i + before)
                        if i > first and branch == "A":
                            turn(i)
                        if branch == "B":
                            n, part = divmod(i - first, SPREAD)
                            project_group(FILL + n // GROUPS, n % GROUPS, part, SPREAD)
                            if part == 0 and 2 <= n < TILES + 2:
                                turn_latents(n - 2)
                        if branch == "C" and i == last - 1:
                            turn_y(0)
                        if i - behind >= first:
                            values(i - behind)
                    if branch == "A":
                        project_group(2, 0)
                    for u in range(last - behind, last):
                        values(u)

                def turn_y(t):
                    pe.wait_ge(y_done, L * NG + y_groups(t))
                    if t == 1:
                        pe.wait_ge(o_summed, L * NG + NG)
                    elif t > 1:
                        pe.wait_ge(yT_done, L * TILES + t)
                    for k in range(KT):
                        last = nc.tensor.transpose(ps[:, y_banks(t) + k // 4, P * (k % 4):P * (k % 4 + 1)],
                                                   y[:, t, P * k:P * (k + 1)], ident[:, :])
                    last.then_inc(y_turned, 1)

                def finish():
                    whi, wlo = zip(weights(7), weights(8))

                    pe.wait_ge(piece_lo, L * NP + NP + 1)
                    for t in range(TILES):
                        if t + 1 < TILES:
                            turn_y(t + 1)
                        pe.wait_ge(yT_done, L * TILES + t + 1)
                        if t >= 2:
                            pe.wait_ge(post_done, L * TILES + t - 1)
                        tok = slice(P * t, P * (t + 1))
                        for k in range(KT):
                            for m, (a, w) in enumerate(((hT_hi, whi), (hT_hi, wlo), (hT_lo, whi))):
                                for b in range(2):
                                    last = nc.tensor.matmul(ps[:, 2 * (t % 2) + b, :], a[:, k, tok], w[b][:, k, :],
                                                            start=(k == 0 and m == 0), stop=(k == KT - 1 and m == 2))
                        last.then_inc(out_done, 1)
                        if t >= 1:
                            turn_x(TILES * (L + 1) + t - 1, t - 1)

                project(0)
                project(1)
                attend("A")
                project(2, 1)
                project(3)
                attend("B")
                up()
                pe.wait_ge(kv_lo, L * KV_STEPS + KV_STEPS)
                pe.wait_ge(uq_lo, L * TILES + TILES)
                attend("C")
                finish()


_INS = ["x", "positions", "pre_norm", "w_in", "q_a_norm", "kv_a_norm", "w_uq", "w_ukv", "sink", "w_o", "post_norm"]


def kernel(**inputs):
    import concourse.bacc as _bacc
    from concourse.bass_utils import run_bass_kernel_spmd as _run

    nc = _bacc.Bacc("TRN2", target_bir_lowering=False, num_devices=1)
    data = {name: np.ascontiguousarray(inputs[name]) for name in _INS}
    data["pre_norm"] = np.concatenate([data["pre_norm"], data["pre_norm"][:1]])
    seq = data["x"].shape[1]
    data["positions"] = np.ascontiguousarray(data["positions"].reshape(seq // P, P).T)
    data["table_a"], data["table_b"] = penalty_tables(seq)
    data["freq"] = rope_frequencies()[None, :]
    data["eye"] = np.eye(P, dtype=np.float32)
    arrays, args = {}, []
    for name, a in data.items():
        arrays[f"in_{name}_dram"] = a
        args.append(nc.dram_tensor(f"in_{name}_dram", a.shape, mybir.dt.from_np(a.dtype), kind="ExternalInput").ap())
    args.append(nc.dram_tensor("out_0_dram", data["x"].shape, F32, kind="ExternalOutput").ap())
    encoder_kernel(nc, *args)
    r = _run(nc, [arrays], core_ids=[0])
    return r.results[0]["out_0_dram"]
```
